# Optimizing a Trainium2 kernel written in Bass

```python
import math
import jax, jax.numpy as jnp
from jax import lax
import numpy as np

D_MODEL = 1024
BATCH = 1
SEQ = 256
DEPTH = 2
DEC_BATCH = 8
DEC_SEQ = 4
PAST_LEN = 1024
PAGE_SIZE = 128

N_EVEN = (DEPTH + 1) // 2
N_ODD = DEPTH // 2
A_WIDTH = D_MODEL // 2
A_GROUPS = 8
CHUNK = 128
B_WIDTH = D_MODEL // 2
CONV_W = 31
C_HEADS = 16
KV_GROUPS = 4
HEAD_DIM = D_MODEL // C_HEADS
HPG = C_HEADS // KV_GROUPS
CMP_BLOCK = 32
CMP_STRIDE = 16
CMP_HID = 2 * HEAD_DIM
SEL_BLOCK = 64
N_SEL = 16
WINDOW = 512
WIN_Q_BLOCK = 128
SEL_Q_BLOCK = 32
N_BUCKETS = 32
MAX_DIST = 128
SCALE = HEAD_DIM ** -0.5
D_FF = ((8 * D_MODEL // 3 + 127) // 128) * 128
EPS = 1e-6
NEG = -1e30
FORCE = 1e6

kernel_name = 'hybrid_gmlp_conformer_nsa_step'

def rmsnorm(x, g):
    xf = x.astype(jnp.float32)
    y = xf * lax.rsqrt(jnp.mean(xf * xf, axis=-1, keepdims=True) + EPS)
    return y.astype(x.dtype) * g

def layernorm(x, g, b):
    xf = x.astype(jnp.float32)
    mu = jnp.mean(xf, axis=-1, keepdims=True)
    var = jnp.mean(jnp.square(xf - mu), axis=-1, keepdims=True)
    return ((xf - mu) * lax.rsqrt(var + EPS)).astype(x.dtype) * g + b

def masked_softmax(logits, mask, axis):
    l = jnp.where(mask, logits.astype(jnp.float32), NEG)
    m = jnp.max(l, axis=axis, keepdims=True)
    e = jnp.where(mask, jnp.exp(l - m), 0.0)
    return e / jnp.maximum(jnp.sum(e, axis=axis, keepdims=True), 1e-30)

def t5_bucket(dist):
    exact = N_BUCKETS // 2
    d = jnp.maximum(dist, 0)
    df = jnp.maximum(d, 1).astype(jnp.float32)
    large = exact + (jnp.log(df / exact) / math.log(MAX_DIST / exact) * (N_BUCKETS - exact)).astype(jnp.int32)
    return jnp.where(d < exact, d, jnp.minimum(large, N_BUCKETS - 1))

def adaln_params(c, w, b):
    m = jax.nn.silu(c) @ w + b
    return jnp.split(m[:, None, :], 9, axis=-1)

def modulate(x, g, shift, scale):
    return rmsnorm(x, g) * (1 + scale) + shift

def ffn_half(x, g, shift, scale, gate, w1, w2):
    a, b = jnp.split(modulate(x, g, shift, scale) @ w1, 2, axis=-1)
    return x + 0.5 * gate * ((jax.nn.silu(a) * b) @ w2)

def chunk_spatial_gate(v, ws, bs):
    B, T, C = v.shape
    Tp = -(-T // CHUNK) * CHUNK
    vp = jnp.pad(v, ((0, 0), (0, Tp - T), (0, 0))).reshape(B, Tp // CHUNK, CHUNK, A_GROUPS, C // A_GROUPS)
    w = ws * jnp.tril(jnp.ones((CHUNK, CHUNK), ws.dtype))
    s = jnp.einsum('gts,bnsgd->bntgd', w, vp) + bs.T[None, None, :, :, None]
    return s.reshape(B, Tp, C)[:, :T]

def even_mix(h, conv_state, w_in, w_out, v_g, ws, bs, cw, cb, ln_g, ln_b):
    zu, zv, za, zg = jnp.split(h @ w_in, [A_WIDTH, 2 * A_WIDTH, 2 * A_WIDTH + B_WIDTH], axis=-1)
    u = jax.nn.gelu(zu)
    v = rmsnorm(jax.nn.gelu(zv), v_g)
    a_out = u * chunk_spatial_gate(v, ws, bs)
    glu = za * jax.nn.sigmoid(zg)
    ctx = jnp.concatenate([conv_state.astype(glu.dtype), glu], axis=1)
    conv = lax.conv_general_dilated(ctx, cw[:, None, :].astype(ctx.dtype), (1,), 'VALID',
                                    dimension_numbers=('NWC', 'WIO', 'NWC'),
                                    feature_group_count=B_WIDTH) + cb
    b_out = jax.nn.silu(layernorm(conv, ln_g, ln_b))
    out = jnp.concatenate([a_out, b_out], axis=-1) @ w_out
    return out, ctx[:, -(CONV_W - 1):], v

def compress(k_full, pe, w1, w2):
    B, Tk = k_full.shape[:2]
    n = (Tk - CMP_BLOCK) // CMP_STRIDE + 1
    ids = jnp.arange(n)[:, None] * CMP_STRIDE + jnp.arange(CMP_BLOCK)[None, :]
    blk = k_full[:, ids] + pe[None, None, :, None, :]
    flat = blk.transpose(0, 1, 3, 2, 4).reshape(B, n, KV_GROUPS, CMP_BLOCK * HEAD_DIM)
    return jax.nn.gelu(flat @ w1) @ w2

def cmp_attend(q, kc, vc, q_pos, table):
    B, Tq = q.shape[:2]
    n = kc.shape[1]
    qg = q.reshape(B, Tq, KV_GROUPS, HPG, HEAD_DIM)
    logits = jnp.einsum('btgpd,bngd->bgptn', qg, kc).astype(jnp.float32) * SCALE
    ends = jnp.arange(n) * CMP_STRIDE + CMP_BLOCK - 1
    dist = q_pos[:, None] - ends[None, :]
    bias = table[t5_bucket(dist)].reshape(Tq, n, KV_GROUPS, HPG).transpose(2, 3, 0, 1)
    p = masked_softmax(logits + bias.astype(jnp.float32), dist >= 0, axis=-1)
    o = jnp.einsum('bgptn,bngd->btgpd', p.astype(vc.dtype), vc).reshape(B, Tq, C_HEADS, HEAD_DIM)
    return o, p

def select_blocks(p, q_pos, n_cmp, nsb):
    cs = jnp.arange(n_cmp) * CMP_STRIDE
    ss = jnp.arange(nsb) * SEL_BLOCK
    ov = jnp.clip(jnp.minimum(cs[:, None] + CMP_BLOCK, ss[None, :] + SEL_BLOCK)
                  - jnp.maximum(cs[:, None], ss[None, :]), 0, None).astype(jnp.float32) / CMP_STRIDE
    imp = jnp.einsum('bgptn,nj->bgtj', p, ov)
    j = jnp.arange(nsb)[None, :]
    cur = (q_pos // SEL_BLOCK)[:, None]
    valid = j * SEL_BLOCK <= q_pos[:, None]
    forced = (j == 0) | (j == cur) | (j == cur - 1)
    imp = jnp.where(valid, jnp.where(forced, FORCE, imp), NEG)
    vals, idx = lax.top_k(imp, min(N_SEL, nsb))
    return idx, vals > 0.5 * NEG

def sel_attend(q, kb, vb, idx, valid, q_pos, table):
    B, Tq = q.shape[:2]
    bi = jnp.arange(B)[:, None, None, None]
    gi = jnp.arange(KV_GROUPS)[None, :, None, None]
    kg = kb[bi, gi, idx]
    vg = vb[bi, gi, idx]
    qg = q.reshape(B, Tq, KV_GROUPS, HPG, HEAD_DIM).transpose(0, 2, 1, 3, 4)
    logits = jnp.einsum('bgtpd,bgtksd->bgtpks', qg, kg).astype(jnp.float32) * SCALE
    kpos = idx[..., None] * SEL_BLOCK + jnp.arange(SEL_BLOCK)
    dist = q_pos[None, None, :, None, None] - kpos
    gi5 = jnp.arange(KV_GROUPS)[None, :, None, None, None]
    bias = jnp.moveaxis(table.reshape(N_BUCKETS, KV_GROUPS, HPG)[t5_bucket(dist), gi5], -1, 3)
    mask = ((dist >= 0) & valid[..., None])[:, :, :, None]
    p = masked_softmax(logits + bias.astype(jnp.float32), mask, axis=(-2, -1))
    o = jnp.einsum('bgtpks,bgtksd->bgtpd', p.astype(vg.dtype), vg)
    return o.transpose(0, 2, 1, 3, 4).reshape(B, Tq, C_HEADS, HEAD_DIM)

def selected_branch(q, kb, vb, idx, valid, q_pos, table):
    B, Tq = q.shape[:2]
    if Tq > SEL_Q_BLOCK and Tq % SEL_Q_BLOCK == 0:
        nb = Tq // SEL_Q_BLOCK
        qs = q.reshape(B, nb, SEL_Q_BLOCK, C_HEADS, HEAD_DIM).swapaxes(0, 1)
        ids = idx.reshape(B, KV_GROUPS, nb, SEL_Q_BLOCK, -1).transpose(2, 0, 1, 3, 4)
        vls = valid.reshape(B, KV_GROUPS, nb, SEL_Q_BLOCK, -1).transpose(2, 0, 1, 3, 4)
        ps = q_pos.reshape(nb, SEL_Q_BLOCK)
        o = lax.map(lambda a: sel_attend(a[0], kb, vb, a[1], a[2], a[3], table), (qs, ids, vls, ps))
        return o.swapaxes(0, 1).reshape(B, Tq, C_HEADS, HEAD_DIM)
    return sel_attend(q, kb, vb, idx, valid, q_pos, table)

def window_attend(q, k, v, q_pos, k_pos, table):
    B, N, Tq = q.shape[:3]
    Tk = k.shape[2]
    qg = q.reshape(B, N, Tq, KV_GROUPS, HPG, HEAD_DIM)
    logits = jnp.einsum('bntgpd,bnsgd->bngpts', qg, k).astype(jnp.float32) * SCALE
    dist = q_pos[:, :, None] - k_pos[:, None, :]
    mask = (dist >= 0) & (dist < WINDOW) & (k_pos[:, None, :] >= 0)
    bias = table[t5_bucket(dist)].reshape(N, Tq, Tk, KV_GROUPS, HPG).transpose(0, 3, 4, 1, 2)
    p = masked_softmax(logits + bias.astype(jnp.float32), mask[:, None, None], axis=-1)
    o = jnp.einsum('bngpts,bnsgd->bntgpd', p.astype(v.dtype), v)
    return o.reshape(B, N, Tq, C_HEADS, HEAD_DIM)

def nsa_mix(h, past_cmp, past_sel, win_buf, q_start, w_in, w_out, qn_g, kn_g, pe, w1, w2, table):
    B, T, _ = h.shape
    GH = KV_GROUPS * HEAD_DIM
    sizes = [C_HEADS * HEAD_DIM] + [GH] * 6 + [3 * C_HEADS]
    parts = jnp.split(h @ w_in, np.cumsum(sizes)[:-1].tolist(), axis=-1)
    q = rmsnorm(parts[0].reshape(B, T, C_HEADS, HEAD_DIM), qn_g)

    def kv_rows(a, b):
        return jnp.stack([a.reshape(B, T, KV_GROUPS, HEAD_DIM), b.reshape(B, T, KV_GROUPS, HEAD_DIM)], axis=2)

    cmp_rows = kv_rows(parts[1], parts[2])
    sel_rows = kv_rows(parts[3], parts[4])
    win_rows = kv_rows(parts[5], parts[6])
    gates = jax.nn.sigmoid(parts[7]).reshape(B, T, 3, C_HEADS, 1)
    q_pos = q_start + jnp.arange(T)
    cmp_full = cmp_rows if past_cmp is None else jnp.concatenate([past_cmp, cmp_rows], axis=1)
    sel_full = sel_rows if past_sel is None else jnp.concatenate([past_sel, sel_rows], axis=1)
    kc = rmsnorm(compress(cmp_full[:, :, 0], pe[0], w1[0], w2[0]), kn_g)
    vc = compress(cmp_full[:, :, 1], pe[1], w1[1], w2[1])
    o_cmp, p_cmp = cmp_attend(q, kc, vc, q_pos, table)
    Tk = sel_full.shape[1]
    nsb = -(-Tk // SEL_BLOCK)
    idx, valid = select_blocks(p_cmp, q_pos, kc.shape[1], nsb)

    def to_blocks(a):
        a = jnp.pad(a, ((0, 0), (0, nsb * SEL_BLOCK - Tk), (0, 0), (0, 0)))
        return a.reshape(B, nsb, SEL_BLOCK, KV_GROUPS, HEAD_DIM).transpose(0, 3, 1, 2, 4)

    kb = to_blocks(rmsnorm(sel_full[:, :, 0], kn_g))
    vb = to_blocks(sel_full[:, :, 1])
    o_sel = selected_branch(q, kb, vb, idx, valid, q_pos, table)
    if win_buf is None:
        nqb = T // WIN_Q_BLOCK
        pad = ((0, 0), (WINDOW, 0), (0, 0), (0, 0))
        ids = jnp.arange(nqb)[:, None] * WIN_Q_BLOCK + jnp.arange(WIN_Q_BLOCK + WINDOW)[None, :]
        kctx = jnp.pad(rmsnorm(win_rows[:, :, 0], kn_g), pad)[:, ids]
        vctx = jnp.pad(win_rows[:, :, 1], pad)[:, ids]
        o_win = window_attend(q.reshape(B, nqb, WIN_Q_BLOCK, C_HEADS, HEAD_DIM), kctx, vctx,
                              q_pos.reshape(nqb, WIN_Q_BLOCK), ids - WINDOW, table).reshape(B, T, C_HEADS, HEAD_DIM)
        ctx = win_rows
    else:
        ctx = jnp.concatenate([win_buf, win_rows], axis=1)
        n_ctx = ctx.shape[1]
        k_pos = (q_start + T - n_ctx + jnp.arange(n_ctx))[None]
        o_win = window_attend(q[:, None], rmsnorm(ctx[:, :, 0], kn_g)[:, None], ctx[:, :, 1][:, None],
                              q_pos[None], k_pos, table)[:, 0]
    new_win = ctx[:, -min(WINDOW, ctx.shape[1]):]
    o = gates[:, :, 0] * o_cmp + gates[:, :, 1] * o_sel + gates[:, :, 2] * o_win
    return o.reshape(B, T, C_HEADS * HEAD_DIM) @ w_out, cmp_rows, sel_rows, new_win

def setup_inputs(seed: int = 0) -> dict:
    key = jax.random.key(seed)
    ks = jax.random.split(key, 32)

    def nrm(k, shape, s=1.0):
        return s * jax.random.normal(k, shape, jnp.float32)

    n_pages = PAST_LEN // PAGE_SIZE
    n_used = DEC_BATCH * n_pages
    n_pool = n_used + (n_used + 3) // 4
    page_table = jax.random.permutation(ks[0], n_pool)[:n_used].reshape(DEC_BATCH, n_pages).astype(jnp.int32)
    w_buf = min(WINDOW, PAST_LEN)
    GH = KV_GROUPS * HEAD_DIM
    nsa_in = C_HEADS * HEAD_DIM + 6 * GH + 3 * C_HEADS
    return {
        'x_prompt': nrm(ks[1], (BATCH, SEQ, D_MODEL)),
        'x_sample': nrm(ks[2], (DEC_BATCH, DEC_SEQ, D_MODEL)),
        'c_prompt': nrm(ks[3], (BATCH, D_MODEL)),
        'c_sample': nrm(ks[4], (DEC_BATCH, D_MODEL)),
        'cache_cmp_kv': nrm(ks[5], (n_pool, PAGE_SIZE, N_ODD, 2, KV_GROUPS, HEAD_DIM)),
        'cache_sel_kv': nrm(ks[6], (n_pool, PAGE_SIZE, N_ODD, 2, KV_GROUPS, HEAD_DIM)),
        'page_table': page_table,
        'state_win_kv': nrm(ks[7], (N_ODD, DEC_BATCH, w_buf, 2, KV_GROUPS, HEAD_DIM)),
        'state_conv': nrm(ks[8], (N_EVEN, DEC_BATCH, CONV_W - 1, B_WIDTH), 0.5),
        'ada_w': nrm(ks[9], (DEPTH, D_MODEL, 9 * D_MODEL), 0.5 * D_MODEL ** -0.5),
        'ada_b': nrm(ks[10], (DEPTH, 9 * D_MODEL), 0.02),
        'norm_g': 1.0 + nrm(ks[11], (DEPTH, 3, D_MODEL), 0.05),
        'ffn_w1': nrm(ks[12], (DEPTH, 2, D_MODEL, 2 * D_FF), D_MODEL ** -0.5),
        'ffn_w2': nrm(ks[13], (DEPTH, 2, D_FF, D_MODEL), D_FF ** -0.5),
        'even_w_in': nrm(ks[14], (N_EVEN, D_MODEL, 2 * A_WIDTH + 2 * B_WIDTH), D_MODEL ** -0.5),
        'even_w_out': nrm(ks[15], (N_EVEN, A_WIDTH + B_WIDTH, D_MODEL), (A_WIDTH + B_WIDTH) ** -0.5),
        'gmlp_v_g': 1.0 + nrm(ks[16], (N_EVEN, A_WIDTH), 0.05),
        'gmlp_ws': nrm(ks[17], (N_EVEN, A_GROUPS, CHUNK, CHUNK), CHUNK ** -0.5),
        'gmlp_bs': 1.0 + nrm(ks[18], (N_EVEN, A_GROUPS, CHUNK), 0.05),
        'conv_w': nrm(ks[19], (N_EVEN, CONV_W, B_WIDTH), CONV_W ** -0.5),
        'conv_b': nrm(ks[20], (N_EVEN, B_WIDTH), 0.02),
        'conv_ln_g': 1.0 + nrm(ks[21], (N_EVEN, B_WIDTH), 0.05),
        'conv_ln_b': nrm(ks[22], (N_EVEN, B_WIDTH), 0.02),
        'nsa_w_in': nrm(ks[23], (N_ODD, D_MODEL, nsa_in), D_MODEL ** -0.5),
        'nsa_w_out': nrm(ks[24], (N_ODD, C_HEADS * HEAD_DIM, D_MODEL), (C_HEADS * HEAD_DIM) ** -0.5),
        'q_norm_g': 1.0 + nrm(ks[25], (N_ODD, HEAD_DIM), 0.05),
        'k_norm_g': 1.0 + nrm(ks[26], (N_ODD, HEAD_DIM), 0.05),
        'cmp_pe': nrm(ks[27], (N_ODD, 2, CMP_BLOCK, HEAD_DIM), 0.1),
        'cmp_w1': nrm(ks[28], (N_ODD, 2, CMP_BLOCK * HEAD_DIM, CMP_HID), (CMP_BLOCK * HEAD_DIM) ** -0.5),
        'cmp_w2': nrm(ks[29], (N_ODD, 2, CMP_HID, HEAD_DIM), CMP_HID ** -0.5),
        'rel_bias': nrm(ks[30], (N_BUCKETS, C_HEADS), 0.2),
    }

def reference(x_prompt, x_sample, c_prompt, c_sample, cache_cmp_kv, cache_sel_kv, page_table, state_win_kv,
              state_conv, ada_w, ada_b, norm_g, ffn_w1, ffn_w2, even_w_in, even_w_out, gmlp_v_g, gmlp_ws,
              gmlp_bs, conv_w, conv_b, conv_ln_g, conv_ln_b, nsa_w_in, nsa_w_out, q_norm_g, k_norm_g, cmp_pe,
              cmp_w1, cmp_w2, rel_bias):
    xp, xs = x_prompt, x_sample
    n_seq = page_table.shape[0]
    cmp_p, cmp_s, sel_p, sel_s, win_p, win_s = [], [], [], [], [], []
    conv_p, conv_s, v_s = [], [], []
    for l in range(DEPTH):
        mp = adaln_params(c_prompt, ada_w[l], ada_b[l])
        ms = adaln_params(c_sample, ada_w[l], ada_b[l])
        xp = ffn_half(xp, norm_g[l, 0], mp[0], mp[1], mp[2], ffn_w1[l, 0], ffn_w2[l, 0])
        xs = ffn_half(xs, norm_g[l, 0], ms[0], ms[1], ms[2], ffn_w1[l, 0], ffn_w2[l, 0])
        hp = modulate(xp, norm_g[l, 1], mp[3], mp[4])
        hs = modulate(xs, norm_g[l, 1], ms[3], ms[4])
        if l % 2 == 0:
            e = l // 2
            prm = (even_w_in[e], even_w_out[e], gmlp_v_g[e], gmlp_ws[e], gmlp_bs[e], conv_w[e], conv_b[e],
                   conv_ln_g[e], conv_ln_b[e])
            zero_hist = jnp.zeros((xp.shape[0], CONV_W - 1, B_WIDTH), xp.dtype)
            op, cst_p, _ = even_mix(hp, zero_hist, *prm)
            os_, cst_s, vrow = even_mix(hs, state_conv[e], *prm)
            conv_p.append(cst_p)
            conv_s.append(cst_s)
            v_s.append(vrow)
        else:
            o = l // 2
            prm = (nsa_w_in[o], nsa_w_out[o], q_norm_g[o], k_norm_g[o], cmp_pe[o], cmp_w1[o], cmp_w2[o], rel_bias)
            past_cmp = cache_cmp_kv[page_table, :, o].reshape(n_seq, -1, 2, KV_GROUPS, HEAD_DIM)
            past_sel = cache_sel_kv[page_table, :, o].reshape(n_seq, -1, 2, KV_GROUPS, HEAD_DIM)
            op, rc_p, rs_p, w_p = nsa_mix(hp, None, None, None, 0, *prm)
            os_, rc_s, rs_s, w_s = nsa_mix(hs, past_cmp, past_sel, state_win_kv[o], past_cmp.shape[1], *prm)
            cmp_p.append(rc_p)
            cmp_s.append(rc_s)
            sel_p.append(rs_p)
            sel_s.append(rs_s)
            win_p.append(w_p)
            win_s.append(w_s)
        xp = xp + mp[5] * op
        xs = xs + ms[5] * os_
        xp = ffn_half(xp, norm_g[l, 2], mp[6], mp[7], mp[8], ffn_w1[l, 1], ffn_w2[l, 1])
        xs = ffn_half(xs, norm_g[l, 2], ms[6], ms[7], ms[8], ffn_w1[l, 1], ffn_w2[l, 1])
    new_cmp_kv_prompt = jnp.stack(cmp_p, axis=2)
    new_cmp_kv_sample = jnp.stack(cmp_s, axis=2)
    new_sel_kv_prompt = jnp.stack(sel_p, axis=2)
    new_sel_kv_sample = jnp.stack(sel_s, axis=2)
    new_win_kv_prompt = jnp.stack(win_p, axis=0)
    new_win_kv_sample = jnp.stack(win_s, axis=0)
    new_conv_prompt = jnp.stack(conv_p, axis=0)
    new_conv_sample = jnp.stack(conv_s, axis=0)
    new_gmlp_v_sample = jnp.stack(v_s, axis=0)
    return (xp, xs, new_cmp_kv_prompt, new_cmp_kv_sample, new_sel_kv_prompt, new_sel_kv_sample,
            new_win_kv_prompt, new_win_kv_sample, new_conv_prompt, new_conv_sample, new_gmlp_v_sample)


_drawn_inputs = setup_inputs


def setup_inputs(seed=0):
    import zlib

    import numpy as np

    out = dict(_drawn_inputs(seed))
    spreads = {}
    factors = {'cache_cmp_kv': 3.03,
     'cache_sel_kv': 6.722,
     'gmlp_bs': 8.0,
     'conv_b': 8.0,
     'conv_ln_g': 7.727,
     'conv_ln_b': 8.0,
     'q_norm_g': 8.0,
     'k_norm_g': 8.0,
     'cmp_pe': 6.635,
     'rel_bias': 5.908}
    for name, (base, spread) in spreads.items():
        noise = np.random.default_rng([zlib.crc32(name.encode()), seed]).standard_normal(out[name].shape)
        drawn = base * np.exp(spread * noise) if base else spread * noise
        out[name] = __import__('jax').numpy.asarray(drawn.astype(out[name].dtype))
    for name, factor in factors.items():
        out[name] = (out[name] * factor).astype(out[name].dtype)
    return out
```

```python
import math
from contextlib import ExitStack

import numpy as np
import concourse.bass as bass
import concourse.mybir as mybir

F32 = mybir.dt.float32
F32R = mybir.dt.float32r
I32 = mybir.dt.int32
ALU = mybir.AluOpType
ACT = mybir.ActivationFunctionType
AX = mybir.AxisListType

P = 128
D = 1024
KD = D // P
NP_, NB, NT = 256, 8, 4
NS = NB * NT
T = NP_ + NS
NC = 1 + NB
DFF = 2816
KF = DFF // P
AW = 512
CW = 31
HD = 64
EPS = 1e-6
NEG = -1e30
UW = 256
W2CUT = [0, 6, 12, 17, 22]
HALF_PAIRS = KF // 2
N_BUCKETS, MAX_DIST = 32, 128
PAST = 1024
WIN = 512
NCMP_S, NCMP_P = 63, 15

FFN_UNITS = KF + 4 * 4
IN0 = FFN_UNITS
OUT0 = IN0 + 8
FFN01 = OUT0 + 4
FFN10 = FFN01 + FFN_UNITS
IN1 = FFN10 + FFN_UNITS
OUT1 = IN1 + 10
FFN11 = OUT1 + 4
UNITS = FFN11 + FFN_UNITS
FFN_BASE = [0, FFN01, FFN10, FFN11]
ADA_UNITS = 3 * D // UW


def bucket(dist):
    exact = N_BUCKETS // 2
    d = np.maximum(dist, 0)
    df = np.maximum(d, 1).astype(np.float32)
    large = exact + (np.log(df / exact) / math.log(MAX_DIST / exact) * (N_BUCKETS - exact)).astype(np.int32)
    return np.where(d < exact, d, np.minimum(large, N_BUCKETS - 1))


C_ID, C_BD, C_UP, C_BLK, C_GRP, C_HALF = 0, 128, 256, 384, 416, 544
C_OH, C_NEW, C_WIN, C_J = 546, 546 + 224, 546 + 224 + 128, 546 + 224 + 132
C_ANTI = C_J + 14
C_COLS = C_ANTI + P
G_TOK, G_HEAD = 0, NB // 2 * NS
G_COLS = G_HEAD + 3 * P
REL = 511


def shape_constants():
    c = np.zeros((P, C_COLS), np.float32)
    i = np.arange(P)
    c[:, C_ID:C_ID + P] = np.eye(P)
    c[:, C_BD:C_BD + P] = i[:, None] // HD == i[None] // HD
    c[:, C_UP:C_UP + P] = i[:, None] <= i[None]
    s = np.arange(NS)
    c[:NS, C_BLK:C_BLK + NS] = (s[:, None] // NT == s[None] // NT) & (s[:, None] <= s[None])
    b2, g, t = i // 64, i // 16 % 4, i // 4 % 4
    c[:, C_GRP:C_GRP + P] = i[:, None] // 4 == i[None] // 4
    c[:, C_HALF] = g % 2 == 0
    c[:, C_HALF + 1] = g % 2 == 1
    dist = [128 + np.arange(NT)[:, None] - np.arange(128)[None],
            np.arange(NT)[:, None] - np.arange(NS)[None] % NT,
            np.full((NT, 1), 4 * MAX_DIST),
            PAST + np.arange(NT)[:, None] - (16 * np.arange(NCMP_S)[None] + 31)]
    dist = np.concatenate(dist, 1)
    c[:, C_OH:C_OH + 224] = (bucket(dist)[:, None] == np.arange(N_BUCKETS)[None, :, None]).reshape(P, 224)
    key_b, key_t = s // NT, s % NT
    for pair in range(4):
        ok = (key_b[None] == 2 * pair + b2[:, None]) & (key_t[None] <= t[:, None])
        c[:, C_NEW + NS * pair:C_NEW + NS * (pair + 1)] = np.where(ok, 0, NEG)
    c[:, C_WIN:C_WIN + 4] = np.where(np.arange(4)[None] > t[:, None], 0, NEG)
    c[:, C_J:C_J + 14] = np.arange(1, 15)
    c[:, C_ANTI:C_ANTI + P] = np.eye(P)[::-1]
    gc = np.zeros((P, G_COLS), np.float32)
    for pair in range(4):
        gc[:, G_TOK + NS * pair:G_TOK + NS * (pair + 1)] = s[None] == ((2 * pair + b2) * NT + t)[:, None]
    for br in range(3):
        gc[:, G_HEAD + P * br:G_HEAD + P * (br + 1)] = i[:, None] == (16 * br + 4 * g + i % 4)[None]
    rel = 255 - np.arange(REL)
    hot = ((bucket(rel)[None] == np.arange(N_BUCKETS)[:, None]) & (rel >= 0)).astype(np.float32)
    causal = np.broadcast_to(np.where(rel >= 0, 0, NEG).astype(np.float32), (16, REL)).copy()
    return c, gc, hot, causal


def emit(nc, a, out):
    with ExitStack() as ctx:
        at = [nc.sbuf_base + (-nc.sbuf_base) % 64]

        def sb(name, shape, dt=F32, where=None):
            size = int(np.prod(shape[1:])) * 4
            spot = where if where is not None else at
            h = nc.alloc_sbuf_tensor_at(name, shape, dt, offset=spot[0])
            spot[0] += size + (-size) % 64
            assert spot[0] <= nc.sbuf_usable_end, (name, spot[0])
            return h

        def sem(name):
            return ctx.enter_context(nc.semaphore(name))

        ps = ctx.enter_context(nc.psum_tensor("ps", [P, 8, 512], F32))

        const = sb("const", [P, C_COLS])
        ones = sb("ones", [P, P])
        vecA = sb("vecA", [P, 144])
        vecB = sb("vecB", [P, 64])
        vecC = sb("vecC", [P, CW * 4])
        cT = sb("cT", [P, KD, 32])
        adaT = sb("adaT", [P, 6, 24, NC])
        xT = sb("xT", [P, KD, T])
        tmp_at = at[0]
        tmp = sb("tmp", [P, KD, T])
        rowt = sb("rowt", [P, 3, T])
        gs = sb("gs", [P, KD, NC])
        mpart = sb("mpart", [P, UW])
        msum = sb("msum", [P, 2, NC])
        xtmp = sb("xtmp", [P, 2, NS])
        h_at = at[0]
        hH = sb("hH", [P, KD, T], F32R)
        hL = sb("hL", [P, KD, T], F32R)
        raw = [sb(f"raw{s}", [P, KD * UW]) for s in range(2)]
        wH = [sb(f"wH{s}", [P, KD * UW], F32R) for s in range(2)]
        wL = [sb(f"wL{s}", [P, KD * UW], F32R) for s in range(2)]
        ada_at = at[0]
        ada = [sb(f"ada{s}", [P, KD, UW]) for s in range(2)]
        ptab = sb("ptab", [1, NB * 8], I32)
        base = at[0]
        spot = [base]
        sa = sb("sa", [P, 2, T], where=spot)
        th = sb("th", [P, 2, T], where=spot)
        hidH = sb("hidH", [P, KF, T], F32R, spot)
        hidL = sb("hidL", [P, KF, T], F32R, spot)
        spot = [base]
        xin = sb("xin", [P, 3, D], where=spot)
        rows = sb("rows", [P, 5, P], where=spot)

        spot = [base + (KF + 2) * T * 8 + 256]
        wT = sb("wT", [P, 8, P], where=spot)
        wS = sb("wS", [NS, 8, NS], where=spot)
        bsT = sb("bsT", [P, 4, P], where=spot)
        cS = sb("cS", [P, 4, NB, 34], where=spot)
        wsn = sb("wsn", [P, 8, P], where=spot)
        stn = sb("stn", [120, 2, AW], where=spot)
        vns = sb("vns", [NS, AW], where=spot)
        cst = sb("cst", [NS, 2, AW], where=spot)
        spot = [base]
        uT, vT, sg = (sb(n, [P, 4, T], where=spot) for n in ("uT", "vT", "sg"))
        cP = sb("cP", [P, 4, 30 + NP_], where=spot)
        acc = sb("acc", [P, 4, T], where=spot)
        prod = sb("prod", [P, 4, NB, CW], where=spot)
        vn = sb("vn", [P, 2, AW], where=spot)
        gS = sb("gS", [P, 4, NS], where=spot)
        DIAGS = 44
        diag = sb("diag", [P, DIAGS, P], where=spot)
        assert spot[0] <= base + (KF + 2) * T * 8 + 256

        LATE_AT = 57344
        spot = [base]
        zT = sb("zT", [P, 20, T], where=spot)
        kvs = sb("kvs", [NS, 12 * P], where=spot)
        KC = sb("KC", [P, NB, 2, 64], where=spot)
        QB = sb("QB", [P, NB, 2, 32], where=spot)
        bias = sb("bias", [P, PAST + NS], where=spot)
        biasc = sb("biasc", [P, 64], where=spot)
        bnew = sb("bnew", [P, 4, NS], where=spot)
        gN = sb("gN", [P, 2, 48], where=spot)
        gR = sb("gR", [P, 4, 3], where=spot)
        KCp = sb("KCp", [P, 4, 16], where=spot)
        vcp = sb("vcp", [NCMP_P, 4, HD], where=spot)
        smallP = sb("smallP", [P, 3, 3, 3], where=spot)
        smallS = sb("smallS", [P, 160], where=spot)
        x_spot = [spot[0]]
        kvn = sb("kvn", [P, 2, 12 * P], where=spot)
        assert spot[0] <= base + LATE_AT, spot[0] - base
        spot = [base + LATE_AT]
        gw = sb("gw", [P, KD, 48], where=spot)
        gcon = sb("gcon", [P, G_COLS], where=spot)
        relr = sb("relr", [16, 512], where=spot)
        table = sb("table", [N_BUCKETS, 16], where=spot)
        TE = sb("TE", [P, P], where=spot)
        w2c = sb("w2c", [P, 2, HD], where=spot)
        perow = sb("perow", [32, P], where=spot)
        peT = sb("peT", [P, 32], where=spot)
        peb = sb("peb", [P, 2], where=spot)
        gk = sb("gk", [P, 2], where=spot)
        nrm = sb("nrm", [P, 12], where=spot)
        reuse = spot[0]
        hotb = sb("hotb", [N_BUCKETS, 512], where=spot)
        causb = sb("causb", [16, 512], where=spot)
        d_spot = [spot[0]]
        gT = sb("gT", [48, T], where=d_spot)
        gm = sb("gm", [P, 4, 3, NS], where=d_spot)
        d_spot = [reuse]
        cre = sb("cre", [P, 4, 4, 2, HD], where=d_spot)
        XTs = [sb(f"XT{i}", [P, 4, 512], where=d_spot) for i in range(2)]
        ksq = sb("ksq", [NCMP_S, 4, HD], where=d_spot)
        kss = sb("kss", [NCMP_S, 12], where=d_spot)
        e_spot = [reuse]
        KS = [sb(f"KS{i}", [P, 528], where=e_spot) for i in range(2)]
        qS = [sb(f"qS{i}", [P, 2, NP_], where=e_spot) for i in range(2)]
        VS = [sb(f"VS{i}", [P, 2, 2, HD], where=e_spot) for i in range(2)]
        VC = [sb(f"VC{i}", [NCMP_P, HD], where=e_spot) for i in range(2)]
        Pp = [sb(f"Pp{i}", [P, 528], where=e_spot) for i in range(3)]
        PT = [sb(f"PT{i}", [P, 512], where=e_spot) for i in range(2)]
        PC = [sb(f"PC{i}", [NCMP_P, P], where=e_spot) for i in range(2)]
        f_spot = [x_spot[0]]
        kr = [sb(f"kr{i}", [P, 12, 256], where=f_spot) for i in range(2)]
        vr = [sb(f"vr{i}", [P, 12, 256], where=f_spot) for i in range(2)]
        assert f_spot[0] <= nc.sbuf_usable_end
        spot = [ada_at]
        w1c = sb("w1c", [P, 2, 16, P], where=spot)
        spot = [ada_at]
        S = sb("S", [P, 1664], where=spot)
        PTs = sb("PTs", [P, 15, P], where=spot)
        spot = [h_at]
        craw = [sb(f"craw{i}", [P, 4, 2, 256], where=spot) for i in range(2)]
        kcn = sb("kcn", [NCMP_S, 4, 2, HD], where=spot)
        assert spot[0] <= h_at + 8 * KD * T
        spot = [h_at]
        Ur = sb("Ur", [P, 16, 256], where=spot)
        spot = [h_at]
        KT = sb("KT", [P, 2, 1536], where=spot)
        QS = sb("QS", [P, 2, 2, 32], where=spot)
        KCs = sb("KCs", [P, 2, 2, 64], where=spot)
        vcs = sb("vcs", [NCMP_S, 2, 4, HD], where=spot)
        spot = [tmp_at]
        vcn = sb("vcn", [NCMP_S, NB, 4, HD], where=spot)
        hid = sb("hid", [P, 4, NCMP_S], where=spot)

        mix_landed = sem("mix_landed")
        const_landed, setup_landed, c_landed, x_landed = (sem(n) for n in ("const_landed", "setup_landed", "c_landed", "x_landed"))
        credits = sem("credits")
        ones_ready = sem("ones_ready")
        rows_turned = sem("rows_turned")
        vecs_ready = sem("vecs_ready")
        cT_ready = sem("cT_ready")
        x_turned = sem("x_turned")
        x_ready = sem("x_ready")
        raw_landed = [sem(f"raw_landed{s}") for s in range(2)]
        hi_done, lo_done, unit_used = sem("hi_done"), sem("lo_done"), sem("unit_used")
        ada_landed = [sem(f"ada_landed{s}") for s in range(2)]
        ada_used, mpart_ready, ada_turned, ada_done = sem("ada_used"), sem("mpart_ready"), sem("ada_turned"), sem("ada_done")
        silu_done, h_done, hidhi_done, hid_done = sem("silu_done"), sem("h_done"), sem("hidhi_done"), sem("hid_done")
        xupd_done, sq_done, ms_ready = sem("xupd_done"), sem("sq_done"), sem("ms_ready")
        var_ready, std_ready = sem("var_ready"), sem("std_ready")
        y_ready, hhi_done, h_ready = sem("y_ready"), sem("hhi_done"), sem("h_ready")
        own = sem("dve_own")
        out_stored, rows_stored = sem("out_stored"), sem("rows_stored")
        ws_turned, ws_ready, st_turned = sem("ws_turned"), sem("ws_ready"), sem("st_turned")
        zin_done, vsq_done, v_ready, v_turned, vn_ready = (sem(n) for n in ("zin_done", "vsq_done", "v_ready", "v_turned", "vn_ready"))
        gate_summed, mix_ready, mixhi_done, mixed = (sem(n) for n in ("gate_summed", "mix_ready", "mixhi_done", "mixed"))
        diag_ready, tap_summed = sem("diag_ready"), sem("tap_summed")
        glu_ready, glu_turned, cst_ready, pad_ready = (sem(n) for n in ("glu_ready", "glu_turned", "cst_ready", "pad_ready"))
        conv_ready, mean_ready, centred, csq_done, ln_ready, lnact_done = (
            sem(n) for n in ("conv_ready", "mean_ready", "centred", "csq_done", "ln_ready", "lnact_done"))

        late_landed, table_landed, w1_landed = sem("late_landed"), sem("table_landed"), sem("w1_landed")
        gates_summed, gate_ready, gate_turned, gates_ready = (sem(n) for n in ("gates_summed", "gate_ready", "gate_turned", "gates_ready"))
        z_done, kv_turned, kv_rows = sem("z_done"), sem("kv_turned"), sem("kv_rows")
        qsq_ready, qsum_ready, qvar_ready, qstd_ready, qn_done = (
            sem(n) for n in ("qsq_ready", "qsum_ready", "qvar_ready", "qstd_ready", "qn_done"))
        pe_turned, pe_copied, peb_summed, peb_ready = (sem(n) for n in ("pe_turned", "pe_copied", "peb_summed", "peb_ready"))
        te_ready, rel_summed, rel_ready, rel_stored, u_landed, bias_summed, bias_ready, qkg_ready = (
            sem(n) for n in ("te_ready", "rel_summed", "rel_ready", "rel_stored", "u_landed", "bias_summed", "bias_ready", "qkg_ready"))
        craw_landed = [sem(f"craw_landed{i}") for i in range(2)]
        cre_ready, cre_turned, xta_ready, xtd_ready, chid_summed, chid_ready, ckv_summed, ckv_taken = (
            sem(n) for n in ("cre_ready", "cre_turned", "xta_ready", "xtd_ready", "chid_summed", "chid_ready", "ckv_summed", "ckv_taken"))
        cvar_ready, cstd_ready, ck_ready, ck_turned, kc_ready = (
            sem(n) for n in ("cvar_ready", "cstd_ready", "ck_ready", "ck_turned", "kc_ready"))
        qb_ready = sem("qb_ready")
        xp_ready = sem("xp_ready")
        group_ready, scored, negmax, exped, scaled, p_turned, pt_ready, pc_ready, o_summed, o_taken = (
            sem(n) for n in ("group_ready", "scored", "negmax", "exped", "scaled", "p_turned", "pt_ready",
                             "pc_ready", "o_summed", "o_taken"))
        k_landed = [sem(f"k_landed{i}") for i in range(2)]
        v_landed = [sem(f"v_landed{i}") for i in range(2)]
        s_small, s_cscored, s_cmax, s_cexp, imp_ready, imp_summed = (
            sem(n) for n in ("s_small", "s_cscored", "s_cmax", "s_cexp", "imp_ready", "imp_summed"))
        s_ksq, s_kvar, s_kstd, s_kn, kt_turned, kt_ready, s_scored, s_added, s_max, s_exp, s_scaled = (
            sem(n) for n in ("s_ksq", "s_kvar", "s_kstd", "s_kn", "kt_turned", "kt_ready", "s_scored", "s_added", "s_max",
                             "s_exp", "s_scaled"))
        s_pturned, s_pready, s_pv, s_o, s_oturned, s_done = (
            sem(n) for n in ("s_pturned", "s_pready", "s_pv", "s_o", "s_oturned", "s_done"))
        ohi_done, o_split = sem("ohi_done"), sem("o_split")
        y_turned, y_rows = sem("y_turned"), sem("y_rows")
        scratch = nc.dram_tensor("relative_bias", (16, 512), F32, kind="Internal").ap()

        ROW_STORES = 2 * 3 + 2 + NB
        LATE = 19
        SETUP_LANDED = 16 * 8
        MIX_LANDED = 16 * (4 + NT * NB)

        ident = const[:, C_ID:C_ID + P]

        w1v = [a["ffn_w1"][l, i].rearrange("(k p) n -> p k n", p=P) for l in range(2) for i in range(2)]
        w2v = [a["ffn_w2"][l, i].rearrange("(k p) n -> p k n", p=P) for l in range(2) for i in range(2)]
        adav = [a["ada_w"][l].rearrange("(k p) n -> p k n", p=P) for l in range(2)]
        y_p, y_s = out[0][0], out[1].rearrange("b t d -> (b t) d")

        ADA_IN_W1 = [1, 3, 5, None]
        ADA_IN_W2 = [2, 4, None, None]
        ada_slot = {}
        uses, count = [0, 0], {}
        order = [0] + [x for f in range(4) for x in (ADA_IN_W1[f], ADA_IN_W2[f]) if x is not None]
        previous = [None, None]
        before = {}
        n = 0
        for third in order:
            for u in range(ADA_UNITS):
                s = u % 2 if third == 0 else 0 if third in ADA_IN_W1 else (0, 1, 0)[u % 3]
                ada_slot[third, u] = s
                uses[s] += 1
                count[third, u] = 16 * uses[s]
                before[third, u] = previous[s]
                previous[s] = n
                n += 1
        first_ada = {third: ADA_UNITS * k for k, third in enumerate(order)}
        assert [order[k] for k in range(6)] == list(range(6))

        SCORE_BANKS = (0, 2, 5)

        def earlier(r):
            return r if r >= 3 else (2, 1, 1)[r]

        ROW_CHUNKS = (12, 13, 14, 15, 8, 9, 16, 17, 10, 11, 18, 19)

        passed = {name: sem(f"passed_{name}") for name in ("sp", "pool", "pe")}

        def hold(eng, name, semaphore, value):
            eng.wait_ge(semaphore, value)
            eng.sem_inc(passed[name], 1)

        block = ctx.enter_context(nc.Block())

        @block.sync
        def _(sp):
            sp.dma_start(const[:, :], a["consts"]).then_inc(const_landed, 16)

            def send(n, parity, src, k, at_=0):
                sp.wait_ge(lo_done, n + 1)
                dst = raw[parity][:, 0:k * UW].rearrange("p (k n) -> p k n", n=UW)
                sp.dma_start(dst, src).then_inc(raw_landed[parity], 16)

            def send_ada(third, u, col, prior):
                s = ada_slot[third, u]
                if prior is not None:
                    sp.wait_ge(ada_used, prior + 1)
                l, part = divmod(third, 3)
                src = adav[l][:, :, bass.ds(col + part * 3 * D, UW)]
                sp.dma_start(ada[s][:, :, :], src).then_inc(ada_landed[s], 16)

            def ffn(f):
                base = FFN_BASE[f]
                t1, t2 = ADA_IN_W1[f], ADA_IN_W2[f]
                if t1 is not None:
                    send_ada(t1, 0, 0, first_ada[t1] - 1)
                with sp.Fori(0, HALF_PAIRS) as j:
                    send(base + 2 * j, 0, w1v[f][:, :, bass.ds(j * UW, UW)], KD)
                    send(base + 2 * j + 1, 1, w1v[f][:, :, bass.ds(j * UW + DFF, UW)], KD)
                    if t1 is not None:
                        send_ada(t1, 0, j * UW + UW, first_ada[t1] + j)
                with sp.Fori(0, 4) as q:
                    for u in range(4):
                        k0, k1 = W2CUT[u], W2CUT[u + 1]
                        send(base + KF + 4 * q + u, u % 2, w2v[f][:, k0:k1, bass.ds(q * UW, UW)], k1 - k0)
                        if u < 3 and t2 is not None:
                            send_ada(t2, u, q * 3 * UW + u * UW, first_ada[t2] + q * 3 + u - (2 if u else 1))

            def startup():
                for u in range(ADA_UNITS):
                    send_ada(0, u, u * UW, before[0, u])

            def even():
                w_in = a["even_w_in"][0].rearrange("(k p) n -> p k n", p=P)
                w_out = a["even_w_out"][0].rearrange("(k p) n -> p k n", p=P)
                for u, col in enumerate((6 * UW, 7 * UW, 4 * UW, 5 * UW, 0, UW, 2 * UW, 3 * UW)):
                    send(IN0 + u, u % 2, w_in[:, :, col:col + UW], KD)
                for u in range(4):
                    send(OUT0 + u, u % 2, w_out[:, :, u * UW:(u + 1) * UW], KD)

            def pages(cache, b, kv, dst, landed, per_page):
                for j in range(8):
                    page = sp.value_load(ptab[0:1, bass.ds(8 * b + j, 1)], min_val=0, max_val=cache.shape[0] - 1)
                    sp.dma_start(dst(j), per_page(cache[bass.ds(page, 1), :, 0, kv])).then_inc(landed, 16)

            def store_rows(dst, src):
                sp.dma_start(dst, src).then_inc(rows_stored, 16)

            def odd():
                w_in = a["nsa_w_in"][0].rearrange("(k p) n -> p k n", p=P)
                w_out = a["nsa_w_out"][0].rearrange("(k p) n -> p k n", p=P)
                sp.wait_ge(ada_used, 6 * ADA_UNITS)
                for v in range(2):
                    sp.dma_start(w1c[:, v, :, :], a["cmp_w1"][0, v].rearrange("(c p) h -> p c h", p=P)).then_inc(w1_landed, 16)
                with sp.Fori(0, 2) as i:
                    for u in range(2):
                        send(IN1 + 2 * i + u, u, w_in[:, :, bass.ds(2 * UW * i + UW * u, UW)], KD)
                for u, part in enumerate((6, 8, 4, 5, 7, 9)):
                    send(IN1 + 4 + u, u % 2, w_in[:, :, part * UW:part * UW + UW], KD)
                for u in range(2):
                    send(OUT1 + u, u, w_out[:, :, u * UW:(u + 1) * UW], KD)
                sp.wait_ge(table_landed, 16)
                sp.wait_ge(z_done, 12)
                with sp.Fori(0, NB) as b:
                    for kv in range(2):
                        hold(sp, "sp", cre_ready, 8 * b + 4 * kv + 4)
                        pages(a["cache_cmp_kv"], b, kv, lambda j: craw[kv][64 * (j % 2):64 * (j % 2) + 64, j // 2],
                              craw_landed[kv], lambda x: x.rearrange("i (q s) g d -> (i q) s (g d)", s=2))
                for t in range(2):
                    sp.wait_ge(kv_rows, t + 1)
                    for br in range(3):
                        rows_ = out[6][0, 0, P * t:P * t + P] if br == 2 else out[2 + 2 * br][0, P * t:P * t + P, 0]
                        store_rows(rows_.rearrange("t v g d -> t (v g d)"), kvn[:, t, 512 * br:512 * br + 512])
                sp.wait_ge(kv_rows, 3)
                for br in range(2):
                    store_rows(out[3 + 2 * br][:, :, 0].rearrange("b t v g d -> (b t) (v g d)"), kvs[:, 512 * br:512 * br + 512])
                for b in range(NB):
                    store_rows(out[7][0, b, WIN - NT:WIN].rearrange("t v g d -> t (v g d)"), kvs[NT * b:NT * b + NT, 1024:1536])
                sp.wait_ge(cre_ready, 8 * NB + 8)
                sp.wait_ge(rel_stored, 16)
                skew = bass.AP(tensor=scratch.tensor, offset=0, ap=[[1, P], [512, 16], [1, 256]])
                sp.dma_start(Ur[:, :, :], skew).then_inc(u_landed, 16)
                sp.wait_ge(rows_stored, 16 * ROW_STORES)
                sp.wait_ge(group_ready, 32)
                with sp.Fori(0, 4) as i:
                    def of_window(b2, kv):
                        win = a["state_win_kv"][0][bass.ds(2 * i + b2, 1)].rearrange("i (n p) v g d -> p (i n) v (g d)", p=P)
                        return win[:, :, kv, :]

                    whole = lambda x: x.rearrange("i p g d -> (i p) (g d)")
                    for b2 in range(2):
                        hold(sp, "sp", kt_turned, 12 * i + 6 * b2 + 6)
                        if b2 == 1:
                            sp.wait_ge(o_taken, 44)
                        pages(a["cache_sel_kv"], 2 * i + b2, 0, lambda j: kr[b2][:, j, :], k_landed[b2], whole)
                        sp.dma_start(kr[b2][:, 8:12, :], of_window(b2, 0)).then_inc(k_landed[b2], 16)
                    hold(sp, "sp", s_pv, i + 1)
                    for b2 in range(2):
                        pages(a["cache_sel_kv"], 2 * i + b2, 1, lambda j: vr[b2][:, j, :], v_landed[b2], whole)
                        sp.dma_start(vr[b2][:, 8:12, :], of_window(b2, 1)).then_inc(v_landed[b2], 16)
                for u in range(2, 4):
                    send(OUT1 + u, u % 2, w_out[:, :, u * UW:(u + 1) * UW], KD)

            startup()
            ffn(0)
            even()
            ffn(1)
            ffn(2)
            odd()
            ffn(3)

        @block.gpsimd
        def _(pool):
            stored = [0]

            def store(dst, src):
                stored[0] += 1
                pool.dma_start(dst, src).then_inc(out_stored, 16)

            def load(dst, src):
                loads[0] += 1
                pool.dma_start(dst, src).then_inc(late_landed, 16)

            def odd():
                pool.wait_ge(h_ready, 6)
                pool.memset(TE[:, :], 0.0).then_inc(te_ready, 1)
                pool.wait_ge(te_ready, 1)
                load(gw[:, :, :], a["nsa_w_in"][0, :, 10 * UW:10 * UW + 48].rearrange("(k p) n -> p k n", p=P))
                load(gcon[:, :], a["gcon"])
                load(hotb[:, 0:REL], a["hot"])
                load(causb[:, 0:REL], a["causal"])
                load(table[:, :], a["rel_bias"])
                load(w2c[:, :, :], a["cmp_w2"][0].rearrange("v h d -> h v d"))
                load(perow[:, :], a["cmp_pe"][0].rearrange("v (c s) d -> (v c) (s d)", s=2))
                for h in range(2):
                    load(gk[64 * h:64 * h + 64, 0:1], a["q_norm_g"].rearrange("e d -> d e"))
                    load(gk[64 * h:64 * h + 64, 1:2], a["k_norm_g"].rearrange("e d -> d e"))
                for t in range(NT):
                    for h in range(2):
                        dst = TE[N_BUCKETS * t:N_BUCKETS * t + N_BUCKETS, 64 * h:64 * h + 64]
                        load(dst.rearrange("b (g t p) -> b g t p", t=NT, p=4)[:, :, t, :],
                             a["rel_bias"].rearrange("b (g p) -> b g p", p=4))
                assert loads[0] == LATE
                pool.sem_inc(cre_ready, 8)
                store(out[7][0, :, 0:WIN - NT], a["state_win_kv"][0, :, NT:WIN])
                pool.wait_ge(kv_rows, 3)
                pool.memset(KCp[:, :, 15:16], 0.0)
                pool.memset(KC[:, :, :, 63:64], 0.0)
                pool.wait_ge(rel_ready, 1)
                pool.dma_start(scratch[:, 0:REL], relr[:, 0:REL]).then_inc(rel_stored, 16)
                pool.wait_ge(gates_ready, 1)
                with pool.Fori(0, NB) as b:
                    for kv in range(2):
                        hold(pool, "pool", craw_landed[kv], P * b + P)
                        for n in range(4):
                            hold(pool, "pool", cre_turned, 8 * b + 4 * kv + n + 1)
                            pool.tensor_copy(cre[:, n, :, :, :],
                                             craw[kv][:, n, :, :].rearrange("q s (g d) -> q g s d", d=HD)).then_inc(cre_ready, 1)
                pool.wait_ge(qn_done, 12)
                pool.wait_ge(kc_ready, 1 + NB)
                pool.wait_ge(ckv_taken, 2 + 2 * NB)
                with pool.Fori(0, 2) as G:
                    for gp in range(2):
                        hold(pool, "pool", o_taken, 16 * G + 8 * gp + 4)
                        for half in range(2):
                            rows_, src = slice(64 * half, 64 * half + 64), slice(64 * gp, 64 * gp + 64)
                            for br in range(2):
                                pool.tensor_copy(KS[gp][rows_, 16 + 256 * br:272 + 256 * br],
                                                 zT[src, bass.ds(8 + 2 * br + G, 1), 0:NP_].rearrange("p i t -> p (i t)")).then_inc(group_ready, 1)
                                hold(pool, "pool", group_ready, 16 * G + 8 * gp + 2 * half + br + 1)
                        pool.tensor_copy(KS[gp][:, 0:16], KCp[:, bass.ds(2 * G + gp, 1), :].rearrange("p i t -> p (i t)")).then_inc(group_ready, 1)
                        pool.tensor_copy(qS[gp][:, :, :], zT[:, bass.ds(4 * G + 2 * gp, 2), 0:NP_]).then_inc(group_ready, 1)
                        v = kvn[:, :, 512:1536].rearrange("p t (b v c) -> p t b v c", b=2, v=2)[:, :, :, 1, :]
                        pool.tensor_copy(VS[gp][:, :, :, :], v[:, :, :, bass.ds(128 * G + 64 * gp, 64)]).then_inc(group_ready, 1)
                        pool.tensor_copy(VC[gp][:, :], vcp[:, bass.ds(2 * G + gp, 1), :].rearrange("p i t -> p (i t)")).then_inc(group_ready, 1)
                        hold(pool, "pool", group_ready, 16 * G + 8 * gp + 8)
                pool.memset(QB[:, :, :, :], 0.0).then_inc(qb_ready, 1)
                pool.wait_ge(qb_ready, 1)
                pool.wait_ge(qn_done, 12)
                copies = 0
                for h in range(2):
                    for G in range(2):
                        for pp in range(2):
                            src = zT[64 * pp:64 * pp + 64, 4 * G + 2 * h:4 * G + 2 * h + 2, NP_:T].rearrange("d c (b t) -> d c b t", t=NT)
                            dst = QB[64 * h:64 * h + 64, :, G, 16 * h:16 * h + 16].rearrange("d b (t c p) -> d c b t p", t=NT, p=2)
                            for c in range(2):
                                pool.tensor_copy(dst[:, c, :, :, pp], src[:, c]).then_inc(qb_ready, 1)
                                copies += 1
                                pool.wait_ge(qb_ready, 1 + copies)
                pool.wait_ge(o_taken, 44)
                with pool.Fori(0, 4) as i:
                    hold(pool, "pool", s_pv, i + 1)
                    pool.tensor_copy(QS[:, :, :, :], QB[:, bass.ds(2 * i, 2), :, :]).then_inc(s_small, 1)
                    pool.tensor_copy(KCs[:, :, :, :], KC[:, bass.ds(2 * i, 2), :, :]).then_inc(s_small, 1)
                    pool.tensor_copy(vcs[:, :, :, :], vcn[:, bass.ds(2 * i, 2), :, :]).then_inc(s_small, 1)

            loads = [0]
            pool.memset(ones[:, :], 1.0).then_inc(ones_ready, 1)
            pool.memset(cT[:, :, :], 0.0).then_inc(ones_ready, 1)
            pool.memset(rows[:, :, :], 0.0).then_inc(ones_ready, 1)
            pool.wait_ge(ones_ready, 3)
            pool.dma_start(rows[0:KD, 4, :], a["c_prompt"].rearrange("b (c p) -> (b c) p", p=P)).then_inc(c_landed, 16)
            pool.dma_start(rows[KD:KD * NC, 4, :], a["c_sample"].rearrange("b (c p) -> (b c) p", p=P)).then_inc(c_landed, 16)
            flat = a["ada_b"].rearrange("l (c p) -> (l c) p", p=P)
            pool.dma_start(rows[:, 0, :], flat[0:P, :]).then_inc(setup_landed, 16)
            pool.dma_start(rows[0:16, 1, :], flat[P:144, :]).then_inc(setup_landed, 16)
            pool.dma_start(rows[0:48, 2, :], a["norm_g"].rearrange("l n (c p) -> (l n c) p", p=P)).then_inc(setup_landed, 16)
            for k, name in enumerate(("gmlp_v_g", "conv_b", "conv_ln_g", "conv_ln_b")):
                pool.dma_start(rows[48 + 4 * k:52 + 4 * k, 2, :], a[name].rearrange("e (c p) -> (e c) p", p=P)).then_inc(setup_landed, 16)
            pool.dma_start(rows[0:4 * CW, 3, :], a["conv_w"][0].rearrange("w (c p) -> (w c) p", p=P)).then_inc(setup_landed, 16)
            pool.dma_start(xin[:, 0:2, :], a["x_prompt"][0].rearrange("(t p) d -> p t d", p=P)).then_inc(x_landed, 16)
            pool.dma_start(xin[0:NS, 2, :], a["x_sample"].rearrange("b t d -> (b t) d")).then_inc(x_landed, 16)
            pool.dma_start(wsn[:, :, :], a["gmlp_ws"][0].rearrange("g t s -> t g s")).then_inc(mix_landed, 16)
            for h in range(2):
                src = a["gmlp_bs"][0, h:8:2, :].rearrange("(i g) t -> i g t", i=1).to_broadcast([64, 4, P])
                pool.dma_start(bsT[64 * h:64 * h + 64, :, :], src).then_inc(mix_landed, 16)
            pool.dma_start(stn[:, :, :], a["state_conv"][0].rearrange("(h b) w c -> (b w) h c", h=2)).then_inc(mix_landed, 16)
            pool.dma_start(ptab[:, :], a["page_table"].rearrange("(i b) j -> i (b j)", i=1)).then_inc(table_landed, 16)
            pool.memset(wS[:, :, :], 0.0).then_inc(ones_ready, 1)
            pool.wait_ge(ones_ready, 4)
            with nc.allow_non_contiguous_dma(reason="eight 4 x 4 blocks for each group"):
                for b in range(NB):
                    for t in range(NT):
                        pool.dma_start(wS[NT * b:NT * b + NT, :, NT * b + t],
                                       a["gmlp_ws"][0, :, t, 0:NT].rearrange("g s -> s g")).then_inc(mix_landed, 16)
            pool.wait_ge(sq_done, 8)
            pool.memset(cP[:, :, 0:30], 0.0).then_inc(pad_ready, 1)
            pool.wait_ge(vecs_ready, 4)
            for m in range(2 * CW):
                c, w = divmod(m, CW)
                if m >= DIAGS:
                    pool.wait_ge(tap_summed, m - DIAGS + 1)
                pool.tensor_scalar(diag[:, m % DIAGS, :], ident, vecC[:, 4 * w + 2 + c:4 * w + 3 + c], None, ALU.mult).then_inc(diag_ready, 1)
            pool.wait_ge(vn_ready, 3)
            pool.dma_start(out[10].rearrange("e b t c -> (e b t) c"), vns[:, :]).then_inc(out_stored, 16)
            pool.dma_start(out[9][0, :, 0:26, :], a["state_conv"][0, :, 4:30, :]).then_inc(out_stored, 16)
            pool.wait_ge(cst_ready, 2)
            pool.dma_start(out[8][0, 0], cst[0:30, 0, :]).then_inc(out_stored, 16)
            for b in range(NB):
                pool.dma_start(out[9][0, b, 26:30, :], cst[NT * b:NT * b + NT, 1, :]).then_inc(out_stored, 16)
            stored[0] = 11
            odd()
            for t in range(3):
                pool.wait_ge(y_rows, t + 1)
                if t < 2:
                    store(y_p[P * t:P * t + P, :], xin[:, t, :])
                else:
                    store(y_s, xin[0:NS, 2, :])
            pool.wait_ge(out_stored, 16 * stored[0])


        @block.scalar
        def _(act):
            def split(n, parity):
                act.wait_ge(raw_landed[parity], (n - parity) * 8 + 16)
                act.wait_ge(unit_used, n + 1)
                nc.scalar.activation(wH[parity][:, :], raw[parity][:, :], ACT.Copy).then_inc(hi_done, 1)

            def take_ada(third, n):
                act.wait_ge(ada_used, n + 1)
                act.wait_ge(ada_turned, n + 1)
                nc.scalar.activation(mpart[:, :], ps[:, 6, 0:UW], ACT.Copy).then_inc(mpart_ready, 1)

            def ffn(f):
                base = FFN_BASE[f]
                t1, t2 = ADA_IN_W1[f], ADA_IN_W2[f]
                with act.Fori(0, HALF_PAIRS) as j:
                    na, J = base + 2 * j, HALF_PAIRS * f + j
                    act.wait_ge(unit_used, na + 3)
                    split(na + 2, 0)
                    act.wait_ge(h_done, J + 1)
                    nc.scalar.activation(sa[:, :, :], ps[:, 0:2, 0:T], ACT.Silu).then_inc(silu_done, 1)
                    if t1 is not None:
                        take_ada(t1, first_ada[t1] + 1 + j)
                    split(na + 3, 1)
                    act.wait_ge(h_done, J + 2)
                    nc.scalar.activation(hidH[:, bass.ds(2 * j, 2), :], th[:, :, :], ACT.Copy).then_inc(hidhi_done, 1)

                def pair(q, last=False):
                    n = base + KF + 4 * q
                    for u in range(4):
                        if u == 3 and f < 3:
                            squares(4 * PAIR_STAGE[f] + q, q)
                        if not last or u < 2:
                            split(n + u + 2, u % 2)
                        if u < 3 and t2 is not None:
                            take_ada(t2, first_ada[t2] + 3 * q + u)

                if f < 3:
                    with act.Fori(0, 4) as q:
                        pair(q)
                else:
                    with act.Fori(0, 3) as q:
                        pair(q)
                    pair(3, True)

            def squares(Q, q):
                act.wait_ge(xupd_done, Q + 3)
                nc.scalar.activation(tmp[:, bass.ds(2 * q, 2), :], xT[:, bass.ds(2 * q, 2), :], ACT.Square).then_inc(sq_done, 1)

            def norm(k):
                act.wait_ge(var_ready, STAT_OF[k] + 1)
                nc.scalar.activation(rowt[:, 1, :], rowt[:, 0, :], ACT.Sqrt).then_inc(std_ready, 1)
                if k == 4:
                    act.wait_ge(pe_turned, 1)
                    nc.scalar.activation(peT[:, :], ps[:, 5, 0:32], ACT.Copy).then_inc(pe_copied, 1)
                if ADA_AFTER_NORM[k] is not None:
                    take_ada(ADA_AFTER_NORM[k], first_ada[ADA_AFTER_NORM[k]])
                for h in range(2):
                    act.wait_ge(y_ready, 2 * k + h + 1)
                    nc.scalar.activation(hH[:, 4 * h:4 * h + 4, :], tmp[:, 4 * h:4 * h + 4, :], ACT.Copy).then_inc(hhi_done, 1)

            def even():
                def take(u, func, dst):
                    act.wait_ge(unit_used, IN0 + u + 3)
                    split(IN0 + u + 2, u % 2)
                    b = 2 * (u % 2)
                    return nc.scalar.activation(dst, ps[:, b:b + 2, 0:T], func)

                for u in range(2):
                    take(u, ACT.Sigmoid, sg[:, 2 * u:2 * u + 2, :]).then_inc(zin_done, 1)
                for u in range(2, 4):
                    act.wait_ge(unit_used, IN0 + u + 3)
                    split(IN0 + u + 2, u % 2)
                for u in range(2):
                    take(4 + u, ACT.Gelu_apprx_tanh, uT[:, 2 * u:2 * u + 2, :]).then_inc(zin_done, 1)
                for u in range(2):
                    take(6 + u, ACT.Gelu_apprx_tanh, vT[:, 2 * u:2 * u + 2, :]).then_inc(zin_done, 1)
                act.wait_ge(zin_done, 8)
                nc.scalar.activation(tmp[:, 0:4, :], vT[:, :, :], ACT.Square).then_inc(vsq_done, 1)
                act.wait_ge(var_ready, STAT_V + 1)
                nc.scalar.activation(rowt[:, 1, :], rowt[:, 0, :], ACT.Sqrt).then_inc(std_ready, 1)
                for t in range(2):
                    act.wait_ge(v_turned, t + 1)
                    nc.scalar.activation(vn[:, t, :], ps[:, 4 + t, :], ACT.Copy).then_inc(vn_ready, 1)
                act.wait_ge(v_turned, 3)
                nc.scalar.activation(vns[:, :], ps[0:NS, 7, :], ACT.Copy).then_inc(vn_ready, 1)
                act.wait_ge(mix_ready, 1)
                nc.scalar.activation(hH[:, 0:4, :], tmp[:, 0:4, :], ACT.Copy).then_inc(mixhi_done, 1)
                act.wait_ge(glu_turned, 1)
                nc.scalar.activation(cst[0:30, 0, :], ps[0:30, 4, :], ACT.Copy).then_inc(cst_ready, 1)
                nc.scalar.activation(cst[:, 1, :], ps[0:NS, 5, :], ACT.Copy).then_inc(cst_ready, 1)
                act.wait_ge(centred, 1)
                nc.scalar.activation(tmp[:, 4:8, :], acc[:, :, :], ACT.Square).then_inc(csq_done, 1)
                act.wait_ge(var_ready, STAT_LN + 1)
                nc.scalar.activation(rowt[:, 1, :], rowt[:, 0, :], ACT.Sqrt).then_inc(std_ready, 1)
                act.wait_ge(ln_ready, 1)
                for c in range(4):
                    nc.scalar.activation(tmp[:, 4 + c, :], acc[:, c, :], ACT.Silu, bias=vecB[:, 60 + c:61 + c],
                                         scale=vecB[:, 56 + c:57 + c]).then_inc(lnact_done, 1)
                act.wait_ge(lnact_done, 4)
                nc.scalar.activation(hH[:, 4:8, :], tmp[:, 4:8, :], ACT.Copy).then_inc(mixhi_done, 1)
                out_stage(OUT0, 1)

            def out_stage(first, stage):
                with act.Fori(0, 2) as i:
                    for u in range(2):
                        squares(4 * stage + 2 * i + u, 2 * i + u)
                        split(first + 2 * i + u + 2, u)

            def odd():
                act.wait_ge(peb_summed, 1)
                nc.scalar.activation(peb[:, :], ps[:, 5, 32:34], ACT.Copy).then_inc(peb_ready, 1)
                act.wait_ge(gates_summed, 1)
                nc.scalar.activation(gT[:, :], ps[0:48, 6, 0:T], ACT.Sigmoid).then_inc(gate_ready, 1)
                with act.Fori(0, 5) as i:
                    for u in range(2):
                        act.wait_ge(unit_used, IN1 + 2 * i + u + 3)
                        split(IN1 + 2 * i + u + 2, u)
                        nc.scalar.activation(zT[:, bass.ds(4 * i + 2 * u, 2), :], ps[:, 2 * u:2 * u + 2, 0:T], ACT.Copy).then_inc(z_done, 1)
                for t in range(3):
                    act.wait_ge(kv_turned, t + 1)
                    b = 3 * (t % 2)
                    if t < 2:
                        nc.scalar.activation(kvn[:, t, :], ps[:, b:b + 3, :].rearrange("p b n -> p (b n)"), ACT.Copy).then_inc(kv_rows, 1)
                    else:
                        nc.scalar.activation(kvs[:, :], ps[0:NS, b:b + 3, :].rearrange("p b n -> p (b n)"), ACT.Copy).then_inc(kv_rows, 1)
                act.wait_ge(bias_summed, 1)
                nc.scalar.activation(bias[:, 0:896], ps[:, 6, 160:161].to_broadcast([P, 896]), ACT.Copy).then_inc(bias_ready, 1)
                nc.scalar.activation(bias[:, 896:1056], ps[:, 6, 0:160], ACT.Copy).then_inc(bias_ready, 1)
                nc.scalar.activation(biasc[:, 0:NCMP_S], ps[:, 6, 161:224], ACT.Copy).then_inc(bias_ready, 1)

                def take_pairs(b, v, done):
                    for n in (0, 2):
                        act.wait_ge(cre_turned, 8 * b + 4 * v + n + 5)
                        act.wait_ge(chid_summed, done)
                        nc.scalar.activation(XTs[v][:, :, P * n:P * n + P], ps[:, n, :].rearrange("p (g q) -> p g q", g=4),
                                             ACT.Copy).then_inc(xta_ready, 1)

                def step(b, v, last, norm_too=False):
                    s_ = 2 * b + v + 2
                    ahead = None if last else (b + 1, v, s_ + 1)
                    if norm_too:
                        act.wait_ge(qvar_ready, 2 * b + v + 1)
                        nc.scalar.activation(rowt[:, 0, :], zT[:, bass.ds(2 * b + v, 1), :].rearrange("p i t -> p (i t)"),
                                             ACT.Square).then_inc(qsq_ready, 1)
                    if v == 0:
                        compressed(s_, 0, NCMP_S, None, b + 1, None, ahead)
                    else:
                        K = KC[:, b:b + 1, :, 0:NCMP_S] if not norm_too else KC[:, bass.ds(b, 1), :, 0:NCMP_S]
                        V = vcn[:, b:b + 1, :, :] if not norm_too else vcn[:, bass.ds(b, 1), :, :]
                        compressed(s_, 1, NCMP_S, V.rearrange("p i g n -> p (i g) n"), b + 1, K.rearrange("p i g n -> p (i g) n"), ahead)
                    if norm_too:
                        act.wait_ge(qvar_ready, 2 * b + v + 2)
                        nc.scalar.activation(rowt[:, 1, :], rowt[:, 1, :], ACT.Sqrt).then_inc(qstd_ready, 1)

                def compressed(s, v, n, V, turned, K, ahead=None):
                    act.wait_ge(chid_summed, s + 1)
                    act.wait_ge(peb_ready, 1)
                    nc.scalar.activation(hid[:, :, 0:n], ps[:, 4, 0:4 * n].rearrange("p (g n) -> p g n", g=4),
                                         ACT.Gelu_apprx_tanh, bias=peb[:, v:v + 1]).then_inc(chid_ready, 1)
                    if v == 1:
                        act.wait_ge(ck_turned, turned + 1)
                        nc.scalar.activation(K, ps[:, 6, 0:512 if n == NCMP_P else 256].rearrange("p (g n) -> p g n", n=128)[:, :, 0:n],
                                             ACT.Copy).then_inc(kc_ready, 1)
                    if ahead is not None:
                        take_pairs(*ahead)
                    act.wait_ge(ckv_summed, s + 1)
                    rows_ = ps[0:n, 5, 0:256].rearrange("p (g d) -> p g d", g=4)
                    if v == 1:
                        nc.scalar.activation(V, rows_, ACT.Copy).then_inc(ckv_taken, 1)
                    else:
                        nc.scalar.activation(ksq[0:n], rows_, ACT.Square).then_inc(ckv_taken, 1)
                        act.wait_ge(cvar_ready, turned + 1)
                        nc.scalar.activation(kss[0:n, 4:8], kss[0:n, 0:4], ACT.Sqrt).then_inc(cstd_ready, 1)

                take_pairs(0, 0, 1)
                compressed(0, 0, NCMP_P, None, 0, None)
                compressed(1, 1, NCMP_P, vcp[:, :, :], 0, KCp[:, :, 0:NCMP_P])
                take_pairs(0, 1, 2)
                with act.Fori(0, NB - 2) as b:
                    step(b, 0, False, True)
                    step(b, 1, False, True)
                step(NB - 2, 0, False)
                step(NB - 2, 1, False)
                step(NB - 1, 0, True)
                step(NB - 1, 1, True)

                def exps(r, G):
                    t, sl = r // 2 % 2, r % 3
                    nk, ncmp = (P, 7) if t == 0 else (2 * P, NCMP_P)
                    act.wait_ge(negmax, 16 * G + r + 1)
                    act.wait_ge(p_turned, 16 * G + earlier(r))
                    b = SCORE_BANKS[sl]
                    for br, (dst, src) in enumerate(((Pp[sl][:, 0:ncmp], ps[:, b, 0:ncmp]), (Pp[sl][:, 16:16 + nk], ps[:, b, 16:16 + nk]),
                                                     (Pp[sl][:, 272:272 + nk], ps[:, b + 1, 16:16 + nk]))):
                        ins = nc.scalar.activation(dst, src, ACT.Exp, bias=smallP[:, sl, 0, br:br + 1],
                                                   accum_out=smallP[:, sl, 1, br:br + 1])
                    ins.then_inc(exped, 1)

                def turned_out(r, G):
                    sl, n = r % 2, 256 if r // 2 % 2 == 0 else 512
                    act.wait_ge(p_turned, 16 * G + r + 3)
                    act.wait_ge(o_summed, 16 * G + r + 1)
                    nc.scalar.activation(PT[sl][:, 0:n], ps[:, 4, 0:n], ACT.Copy).then_inc(pt_ready, 1)

                with act.Fori(0, 2) as G:
                    exps(0, G)
                    exps(1, G)
                    for r in range(16):
                        turned_out(r, G)
                        if r < 14:
                            exps(r + 2, G)

                def squares_of_keys(i, b2):
                    act.wait_ge(k_landed[b2], 144 * i + 144)
                    act.wait_ge(s_scored, 2 * i + 1)
                    nc.scalar.activation(KT[:, :, :].rearrange("p g n -> p (g n)"), kr[b2][:, :, :].rearrange("p n c -> p (n c)"),
                                         ACT.Square).then_inc(s_ksq, 1)

                def roots_of_keys(i, b2):
                    act.wait_ge(s_kvar, 2 * i + b2 + 1)
                    nc.scalar.activation(smallS[:, 64:112], smallS[:, 16:64], ACT.Sqrt).then_inc(s_kstd, 1)

                def pair(i, last=False):
                    for b2 in range(2):
                        for k in range(6):
                            act.wait_ge(kt_turned, 12 * i + 6 * b2 + k + 13)
                            if k == 0:
                                act.wait_ge(s_scored, 2 * i + b2 + 1)
                            nc.scalar.activation(KT[:, k // 3, 512 * (k % 3):512 * (k % 3) + 512], ps[:, 4 + k % 2, :], ACT.Copy).then_inc(kt_ready, 1)
                        if b2 == 0:
                            act.wait_ge(s_cmax, i + 1)
                            nc.scalar.activation(S[:, 1600:1663], S[:, 1600:1663], ACT.Exp, bias=smallS[:, 0:1],
                                                 accum_out=smallS[:, 1:2]).then_inc(s_cexp, 1)
                    act.wait_ge(s_max, 2 * i + 1)
                    nc.scalar.activation(S[:, 1056:1600], S[:, 1056:1600], ACT.Exp, bias=smallS[:, 4:5], accum_out=smallS[:, 6:7]).then_inc(s_exp, 1)
                    act.wait_ge(s_max, 2 * i + 2)
                    nc.scalar.activation(S[:, 0:1056], S[:, 0:1056], ACT.Exp, bias=smallS[:, 3:4], accum_out=smallS[:, 5:6]).then_inc(s_exp, 1)
                    for k in range(4):
                        if k == 2 and not last:
                            squares_of_keys(i + 1, 0)
                        act.wait_ge(s_pturned, 4 * i + k + 1)
                        if k < 3:
                            nc.scalar.activation(PTs[:, 4 * k:4 * k + 4, :], ps[:, 4 + k % 2, :].rearrange("p (n q) -> p n q", n=4), ACT.Copy).then_inc(s_pready, 1)
                        else:
                            nc.scalar.activation(PTs[0:NS, 12:14, :], ps[0:NS, 5, 0:256].rearrange("p (n q) -> p n q", n=2), ACT.Copy).then_inc(s_pready, 1)
                            nc.scalar.activation(PTs[0:NCMP_S, 14, :], ps[0:NCMP_S, 5, 256:384], ACT.Copy).then_inc(s_pready, 1)
                    if not last:
                        roots_of_keys(i + 1, 0)
                        squares_of_keys(i + 1, 1)
                        roots_of_keys(i + 1, 1)

                for b2 in range(2):
                    squares_of_keys(0, b2)
                    roots_of_keys(0, b2)
                with act.Fori(0, 3) as i:
                    pair(i)
                pair(3, True)
                act.wait_ge(s_done, 4)
                for h in range(2):
                    nc.scalar.activation(hH[:, 4 * h:4 * h + 4, :], zT[:, 4 * h:4 * h + 4, :], ACT.Copy).then_inc(ohi_done, 1)
                out_stage(OUT1, 4)

            def results():
                for t in range(3):
                    n = P if t < 2 else NS
                    act.wait_ge(y_turned, t + 1)
                    b = 2 * (t % 2)
                    nc.scalar.activation(xin[0:n, t, :], ps[0:n, b:b + 2, :].rearrange("p b n -> p (b n)"), ACT.Copy).then_inc(y_rows, 1)

            act.sem_inc(exped, 2)
            act.sem_inc(pt_ready, 2)
            act.sem_inc(kt_ready, 2)
            act.sem_inc(silu_done, 1)
            act.sem_inc(mpart_ready, 1)
            act.wait_ge(rows_turned, 1)
            act.wait_ge(ones_ready, 3)
            nc.scalar.activation(cT[:, :, 0:NC], ps[:, 4, 0:KD * NC].rearrange("p (i k) -> p k i", k=KD), ACT.Silu).then_inc(cT_ready, 1)
            for u in range(ADA_UNITS):
                take_ada(0, u)
                c = u - 3
                if 0 <= c < KD:
                    act.wait_ge(x_turned, c + 1)
                    nc.scalar.activation(xT[:, c, :], ps[:, c % 4, 0:T], ACT.Copy).then_inc(x_ready, 1)
            act.wait_ge(x_ready, KD)
            for q in range(4):
                nc.scalar.activation(tmp[:, 2 * q:2 * q + 2, :], xT[:, 2 * q:2 * q + 2, :], ACT.Square).then_inc(sq_done, 1)
            split(0, 0)
            norm(0)
            split(1, 1)
            ffn(0)
            norm(1)
            even()
            norm(2)
            ffn(1)
            norm(3)
            ffn(2)
            norm(4)
            odd()
            norm(5)
            ffn(3)
            results()

        @block.vector
        def _(dve):
            seen = [0]

            def link(ins):
                seen[0] += 1
                ins.then_inc(own, 1)
                dve.wait_ge(own, seen[0])

            class Links:
                def __init__(self, i, per, rounds):
                    self.i, self.per, self.rounds, self.k, self.start = i, per, rounds, 0, seen[0]

                def __call__(self, ins):
                    self.k += 1
                    ins.then_inc(own, 1)
                    dve.wait_ge(own, self.start + self.per * self.i + self.k)

                def end(self):
                    assert self.k == self.per, self.k
                    seen[0] = self.start + self.per * self.rounds

            def lower(n, parity):
                dve.wait_ge(hi_done, n + 1)
                nc.vector.tensor_tensor(wL[parity][:, :], raw[parity][:, :], wH[parity][:, :].bitcast(F32),
                                        ALU.subtract).then_inc(lo_done, 1)

            def finish_ada(third, u, n, ln):
                dve.wait_ge(ada_turned, n + 2)
                ln(nc.vector.tensor_reduce(msum[:, :, :],
                                           ps[:, 7, 0:256].rearrange("p (c j i) -> p c i j", c=2, j=4)[:, :, 0:NC, :],
                                           AX.X, ALU.add))
                bias = vecA[:, bass.ds(third * 24 + 2 * u, 2)].rearrange("p (c i) -> p c i", i=1).to_broadcast([P, 2, NC])
                dst = adaT[:, third, bass.ds(2 * u, 2), :]
                nc.vector.tensor_tensor(dst, msum[:, :, :], bias, ALU.add).then_inc(ada_done, 1)

            def pair_update(third, q, banks, n_last, ln):
                dve.wait_ge(unit_used, n_last + 3)
                g = adaT[:, third, :, :]
                for t in range(2):
                    x = xT[:, bass.ds(2 * q + t, 1), :]
                    ins = nc.vector.scalar_tensor_tensor(out=x[:, 0, 0:NP_], in0=ps[:, banks + t, 0:NP_],
                                                         scalar=g[:, bass.ds(16 + 2 * q + t, 1), 0],
                                                         in1=x[:, 0, 0:NP_], op0=ALU.mult, op1=ALU.add)
                dve.wait_ge(xupd_done, 4 * third + q + 2)
                gb = g[:, bass.ds(16 + 2 * q, 2), 1:NC].rearrange("p c (b t) -> p c b t", t=1).to_broadcast([P, 2, NB, NT])
                ln(nc.vector.tensor_tensor(xtmp[:, :, :].rearrange("p c (b t) -> p c b t", t=NT),
                                           ps[:, banks:banks + 2, NP_:T].rearrange("p c (b t) -> p c b t", t=NT), gb, ALU.mult))
                xs = xT[:, bass.ds(2 * q, 2), NP_:T]
                nc.vector.tensor_tensor(xs, xtmp[:, :, :], xs, ALU.add).then_inc(xupd_done, 1)

            def norm(k, ffn_gate):
                l, part = divmod(k, 3)
                A = adaT[:, k, :, :]
                dve.wait_ge(ms_ready, STAT_OF[k] + 1)
                nc.vector.tensor_scalar(rowt[:, 0, :], ps[:, 7, 0:T], 1.0 / D, EPS, ALU.mult, ALU.add).then_inc(var_ready, 1)
                dve.wait_ge(ada_done, ADA_UNITS * (k + 1) + 1)
                g = vecB[:, (3 * l + part) * 8:(3 * l + part) * 8 + 8].rearrange("p (c i) -> p c i", i=1).to_broadcast([P, KD, NC])
                nc.vector.scalar_tensor_tensor(out=gs[:, :, :], in0=A[:, 8:16, :], scalar=1.0, in1=g, op0=ALU.add, op1=ALU.mult)
                if ffn_gate:
                    nc.vector.tensor_scalar(A[:, 16:24, :], A[:, 16:24, :], 0.5, None, ALU.mult)
                dve.wait_ge(std_ready, STAT_OF[k] + 1)
                link(nc.vector.reciprocal(rowt[:, 2, :], rowt[:, 1, :]))
                for h in range(2):
                    c0, c1 = 4 * h, 4 * h + 4
                    y = tmp[:, c0:c1, :]
                    r = rowt[:, 2:3, :].to_broadcast([P, 4, T])
                    link(nc.vector.tensor_tensor(y, xT[:, c0:c1, :], r, ALU.mult))
                    for c in range(c0, c1):
                        nc.vector.tensor_scalar(tmp[:, c, 0:NP_], tmp[:, c, 0:NP_], gs[:, c, 0:1], A[:, c, 0:1],
                                                ALU.mult, ALU.add)
                    ys = y[:, :, NP_:T].rearrange("p c (b t) -> p c b t", t=NT)
                    wide = lambda v: v.rearrange("p c (b t) -> p c b t", t=1).to_broadcast([P, 4, NB, NT])
                    link(nc.vector.tensor_tensor(ys, ys, wide(gs[:, c0:c1, 1:NC]), ALU.mult))
                    nc.vector.tensor_tensor(ys, ys, wide(A[:, c0:c1, 1:NC]), ALU.add).then_inc(y_ready, 1)
                for h in range(2):
                    dve.wait_ge(hhi_done, 2 * k + h + 1)
                    nc.vector.tensor_tensor(hL[:, 4 * h:4 * h + 4, :], tmp[:, 4 * h:4 * h + 4, :],
                                            hH[:, 4 * h:4 * h + 4, :].bitcast(F32), ALU.subtract).then_inc(h_ready, 1)
                if ADA_AFTER_NORM[k] is not None:
                    finish_ada(ADA_AFTER_NORM[k], 0, first_ada[ADA_AFTER_NORM[k]], link)

            def ffn(f):
                base = FFN_BASE[f]
                t1, t2 = ADA_IN_W1[f], ADA_IN_W2[f]
                with dve.Fori(0, HALF_PAIRS) as j:
                    ln = Links(j, 1, HALF_PAIRS) if t1 is not None else None
                    na, J = base + 2 * j, HALF_PAIRS * f + j
                    lower(na + 2, 0)
                    dve.wait_ge(unit_used, na + 4)
                    dve.wait_ge(silu_done, J + 2)
                    dve.wait_ge(hid_done, J + 1)
                    nc.vector.tensor_tensor(th[:, :, :], ps[:, 2:4, 0:T], sa[:, :, :], ALU.mult).then_inc(h_done, 1)
                    lower(na + 3, 1)
                    if t1 is not None:
                        finish_ada(t1, j + 1, first_ada[t1] + 1 + j, ln)
                        ln.end()
                    dve.wait_ge(hidhi_done, J + 1)
                    nc.vector.tensor_tensor(hidL[:, bass.ds(2 * j, 2), :], th[:, :, :],
                                            hidH[:, bass.ds(2 * j, 2), :].bitcast(F32), ALU.subtract).then_inc(hid_done, 1)

                def pair(q, bank, ln, last=False):
                    n = base + KF + 4 * q
                    for u in range(4):
                        if u == 3:
                            pair_update(NORM_OF[f], q, bank, n + 3, ln)
                        if not last or u < 2:
                            lower(n + u + 2, u % 2)
                        if u < 3 and t2 is not None:
                            finish_ada(t2, 3 * q + u, first_ada[t2] + 3 * q + u, ln)

                per = (4 if t2 is not None else 1)
                if f < 3:
                    with dve.Fori(0, 2) as qq:
                        ln = Links(qq, 2 * per, 2)
                        pair(2 * qq, 4, ln)
                        pair(2 * qq + 1, 0, ln)
                        ln.end()
                else:
                    with dve.Fori(0, 1) as qq:
                        ln = Links(qq, 2 * per, 1)
                        pair(2 * qq, 4, ln)
                        pair(2 * qq + 1, 0, ln)
                        ln.end()
                    pair(2, 4, link)
                    pair(3, 0, link, True)

            def root(r, scale):
                dve.wait_ge(ms_ready, r + 1)
                nc.vector.tensor_scalar(rowt[:, 0, :], ps[:, 7, 0:T], scale, EPS, ALU.mult, ALU.add).then_inc(var_ready, 1)
                dve.wait_ge(std_ready, r + 1)
                link(nc.vector.reciprocal(rowt[:, 2, :], rowt[:, 1, :]))

            def even():
                def taps(w0, w1):
                    start = seen[0]
                    with dve.Fori(w0, w1) as w:
                        for c in range(2):
                            dve.wait_ge(own, start + 2 * w - 2 * w0 + c - 1)
                            nc.vector.scalar_tensor_tensor(out=acc[:, c, 0:NP_], in0=cP[:, c, bass.ds(w, NP_)],
                                                           scalar=vecC[:, bass.ds(4 * w + c, 1)], in1=acc[:, c, 0:NP_],
                                                           op0=ALU.mult, op1=ALU.add).then_inc(own, 1)
                    seen[0] += 2 * (w1 - w0)

                def sample_tap(t):
                    link(nc.vector.tensor_tensor(prod[:, :, :, :], cS[:, :, :, t:t + CW], sample_taps, ALU.mult))
                    link(nc.vector.tensor_reduce(accs[:, :, :, t], prod[:, :, :, :], AX.X, ALU.add))

                sample_taps = vecC[:, :].rearrange("p (w c i) -> p c i w", c=4, i=1).to_broadcast([P, 4, NB, CW])
                accs = acc[:, :, NP_:T].rearrange("p c (b t) -> p c b t", t=NT)
                for u in range(4):
                    lower(IN0 + u + 2, u % 2)
                    if u >= 2:
                        q, b = u - 2, 2 * (u % 2)
                        dve.wait_ge(unit_used, IN0 + u + 3)
                        dve.wait_ge(zin_done, 4)
                        c = slice(2 * q, 2 * q + 2)
                        nc.vector.tensor_tensor(cP[:, c, 30:30 + NP_], ps[:, b:b + 2, 0:NP_], sg[:, c, 0:NP_], ALU.mult).then_inc(glu_ready, 1)
                        nc.vector.tensor_tensor(gS[:, c, :], ps[:, b:b + 2, NP_:T], sg[:, c, NP_:T], ALU.mult).then_inc(glu_ready, 1)
                dve.wait_ge(glu_ready, 4)
                link(nc.vector.tensor_copy(cS[:, :, :, 30:34], gS[:, :, :].rearrange("p c (b t) -> p c b t", t=NT)))
                sample_tap(0)
                lower(IN0 + 6, 0)
                sample_tap(1)
                sample_tap(2)
                lower(IN0 + 7, 1)
                sample_tap(3)
                cb = vecB[:, 52:56].rearrange("p (c i) -> p c i", i=1).to_broadcast([P, 4, NS])
                nc.vector.tensor_tensor(acc[:, :, NP_:T], acc[:, :, NP_:T], cb, ALU.add)
                dve.wait_ge(pad_ready, 1)
                for c in range(2):
                    nc.vector.tensor_scalar(acc[:, c, 0:NP_], cP[:, c, 0:NP_], vecC[:, c:c + 1], vecB[:, 52 + c:53 + c],
                                            ALU.mult, ALU.add).then_inc(own, 1)
                seen[0] += 2
                taps(1, 6)
                lower(IN0 + 8, 0)
                taps(6, 9)
                lower(IN0 + 9, 1)
                root(STAT_V, 1.0 / AW)
                dve.wait_ge(zin_done, 8)
                for c in range(4):
                    nc.vector.scalar_tensor_tensor(out=vT[:, c, :], in0=vT[:, c, :], scalar=vecB[:, 48 + c:49 + c],
                                                   in1=rowt[:, 2, :], op0=ALU.mult, op1=ALU.mult).then_inc(v_ready, 1)
                taps(9, CW)
                dve.wait_ge(tap_summed, 2 * CW)
                for c in range(2):
                    nc.vector.tensor_scalar(acc[:, 2 + c, 0:NP_], ps[:, 6, NP_ * c:NP_ * c + NP_], vecB[:, 54 + c:55 + c], None, ALU.add)
                dve.wait_ge(own, seen[0])
                nc.vector.tensor_copy(xtmp[:, 0, 0:1], acc[:, 1, 0:1]).then_inc(conv_ready, 1)
                dve.wait_ge(gate_summed, 1)
                ps4 = ps[:, 0:4, 0:NP_].rearrange("p c (n t) -> p c n t", t=P)
                bias = bsT[:, :, :].rearrange("p c (n t) -> p c n t", n=1).to_broadcast([P, 4, 2, P])
                link(nc.vector.tensor_tensor(tmp[:, 0:4, 0:NP_].rearrange("p c (n t) -> p c n t", t=P), ps4, bias, ALU.add))
                bias = bsT[:, :, 0:NT].rearrange("p c (n t) -> p c n t", n=1).to_broadcast([P, 4, NB, NT])
                link(nc.vector.tensor_tensor(tmp[:, 0:4, NP_:T].rearrange("p c (b t) -> p c b t", t=NT),
                                             ps[:, 0:4, NP_:T].rearrange("p c (b t) -> p c b t", t=NT), bias, ALU.add))
                nc.vector.tensor_tensor(tmp[:, 0:4, :], tmp[:, 0:4, :], uT[:, :, :], ALU.mult).then_inc(mix_ready, 1)
                dve.wait_ge(mixhi_done, 1)
                nc.vector.tensor_tensor(hL[:, 0:4, :], tmp[:, 0:4, :], hH[:, 0:4, :].bitcast(F32), ALU.subtract).then_inc(mixed, 1)
                dve.wait_ge(mean_ready, 1)
                link(nc.vector.tensor_scalar(rowt[:, 2, :], ps[:, 7, 0:T], 1.0 / AW, None, ALU.mult))
                nc.vector.tensor_tensor(acc[:, :, :], acc[:, :, :], rowt[:, 2:3, :].to_broadcast([P, 4, T]), ALU.subtract).then_inc(centred, 1)
                root(STAT_LN, 1.0 / AW)
                nc.vector.tensor_tensor(acc[:, :, :], acc[:, :, :], rowt[:, 2:3, :].to_broadcast([P, 4, T]), ALU.mult).then_inc(ln_ready, 1)
                dve.wait_ge(mixhi_done, 2)
                nc.vector.tensor_tensor(hL[:, 4:8, :], tmp[:, 4:8, :], hH[:, 4:8, :].bitcast(F32), ALU.subtract).then_inc(mixed, 1)
                out_stage(1, OUT0)

            def out_stage(third, first):
                with dve.Fori(0, 2) as i:
                    ln = Links(i, 2, 2)
                    for u in range(2):
                        pair_update(third, 2 * i + u, 4 - 4 * u, first + 2 * i + u, ln)
                        lower(first + 2 * i + u + 2, u)
                    ln.end()

            def odd():
                dve.wait_ge(late_landed, 16 * LATE)
                nc.vector.memset(nrm[:, 8:12], 1.0)
                link(nc.vector.scalar_tensor_tensor(out=nrm[:, 0:8], in0=gk[:, 0:1].to_broadcast([P, 8]), scalar=HD ** -0.5,
                                                    in1=gk[:, 1:2].to_broadcast([P, 8]), op0=ALU.mult, op1=ALU.mult))
                with dve.Fori(0, 5) as i:
                    for u in range(2):
                        lower(IN1 + 2 * i + u + 2, u)
                dve.wait_ge(gate_turned, 1)
                nc.vector.tensor_copy(gN[:, :, :], ps[:, 6, 0:96].rearrange("p (t c) -> p t c", t=2))
                for pair in range(4):
                    tok = gcon[:, G_TOK + NS * pair:G_TOK + NS * pair + NS].rearrange("p (i t) -> p i t", i=1).to_broadcast([P, 3, NS])
                    ins = nc.vector.tensor_tensor(gm[:, pair, :, :], ps[:, 6, 128:224].rearrange("p (b t) -> p b t", b=3), tok, ALU.mult)
                link(ins)
                nc.vector.tensor_reduce(gR[:, :, :], gm[:, :, :, :], AX.X, ALU.add).then_inc(gates_ready, 1)
                dve.wait_ge(rel_summed, 1)
                nc.vector.tensor_tensor(relr[:, 0:REL], ps[0:16, 7, 0:REL], causb[:, 0:REL], ALU.add).then_inc(rel_ready, 1)
                dve.wait_ge(bias_ready, 2)
                b = bias[:, PAST:PAST + NS].rearrange("p (i t) -> p i t", i=1).to_broadcast([P, 4, NS])
                link(nc.vector.tensor_tensor(bnew[:, :, :], b, const[:, C_NEW:C_NEW + 4 * NS].rearrange("p (i t) -> p i t", i=4), ALU.add))
                xp = XTs[1][:, 0:2, :].rearrange("p a (b n) -> p (a b) n", n=P)
                for s_ in range(2):
                    for gp in range(2):
                        ins = nc.vector.tensor_copy(xp[64 * s_:64 * s_ + 64, gp:8:2, :],
                                                    zT[64 * gp:64 * gp + 64, 12:16, s_:NP_:2])
                ins.then_inc(xp_ready, 1)

                def key_norm(turned, s, n, copies, ln):
                    dve.wait_ge(ckv_taken, s + 1)
                    ln(nc.vector.tensor_reduce(kss[0:n, 0:4], ksq[0:n], AX.X, ALU.add))
                    nc.vector.tensor_scalar(kss[0:n, 0:4], kss[0:n, 0:4], 1.0 / HD, EPS, ALU.mult, ALU.add).then_inc(cvar_ready, 1)
                    dve.wait_ge(cstd_ready, turned + 1)
                    ln(nc.vector.reciprocal(kss[0:n, 8:12], kss[0:n, 4:8]))
                    r = kss[0:n, 8:12].rearrange("p (g i) -> p g i", i=1).to_broadcast([n, 4, HD])
                    for i in range(copies):
                        dst = kcn[0:n, :, i, :] if copies == 2 else kcn[0:n, 0:2, :, :].rearrange("p a b d -> p (a b) d")
                        ins = nc.vector.tensor_tensor(dst, ps[0:n, 5, 0:256].rearrange("p (g d) -> p g d", g=4), r, ALU.mult)
                    ins.then_inc(ck_ready, 1)

                def take_pairs(b, v, done):
                    for n in (1, 3):
                        dve.wait_ge(cre_turned, 8 * b + 4 * v + n + 5)
                        dve.wait_ge(chid_summed, done)
                        nc.vector.tensor_copy(XTs[v][:, :, P * n:P * n + P], ps[:, n, :].rearrange("p (g q) -> p g q", g=4)).then_inc(xtd_ready, 1)

                def norm_chunk(m, ln):
                    dve.wait_ge(qsum_ready, m + 1)
                    nc.vector.tensor_scalar(rowt[:, 1, :], ps[:, 7, 0:T], 1.0 / HD, EPS, ALU.mult, ALU.add).then_inc(qvar_ready, 1)
                    dve.wait_ge(qstd_ready, m + 1)
                    ln(nc.vector.reciprocal(rowt[:, 2, :], rowt[:, 1, :]))
                    z = zT[:, bass.ds(m, 1), :].rearrange("p i t -> p (i t)")
                    nc.vector.scalar_tensor_tensor(out=z, in0=z, scalar=nrm[:, bass.ds(m, 1)], in1=rowt[:, 2, :],
                                                   op0=ALU.mult, op1=ALU.mult).then_inc(qn_done, 1)

                def step(b, v, last, ln, norm_too=False):
                    s_ = 2 * b + v + 2
                    if not last:
                        take_pairs(b + 1, v, s_ + 1)
                    if v == 0:
                        dve.wait_ge(ck_turned, b + 1)
                        key_norm(b + 1, s_, NCMP_S, 1, ln)
                    if norm_too:
                        norm_chunk(2 * b + v, ln)

                take_pairs(0, 0, 1)
                key_norm(0, 0, NCMP_P, 2, link)
                take_pairs(0, 1, 2)
                with dve.Fori(0, NB - 2) as b:
                    ln = Links(b, 4, NB - 2)
                    step(b, 0, False, ln, True)
                    step(b, 1, False, ln, True)
                    ln.end()
                step(NB - 2, 0, False, link)
                step(NB - 2, 1, False, link)
                step(NB - 1, 0, True, link)
                step(NB - 1, 1, True, link)

                def maxima(r, G, ln):
                    t, sl = r // 2 % 2, r % 3
                    nk, ncmp = (P, 7) if t == 0 else (2 * P, NCMP_P)
                    dve.wait_ge(scored, 16 * G + r + 1)
                    mx = smallP[:, sl, 2, :]
                    nc.vector.tensor_reduce(mx[:, 0:1], ps[:, SCORE_BANKS[sl], 0:ncmp], AX.X, ALU.max)
                    ln(nc.vector.tensor_reduce(mx[:, 1:3], ps[:, SCORE_BANKS[sl]:SCORE_BANKS[sl] + 2, 16:16 + nk], AX.X, ALU.max))
                    nc.vector.tensor_scalar(smallP[:, sl, 0, :], mx, -1e20, -1.0, ALU.max, ALU.mult).then_inc(negmax, 1)

                def scale(r, G, ln):
                    t, sl = r // 2 % 2, r % 3
                    nk, ncmp = (P, 7) if t == 0 else (2 * P, NCMP_P)
                    dve.wait_ge(exped, 16 * G + r + 3)
                    f = smallP[:, sl, 2, :]
                    ln(nc.vector.tensor_scalar(f, smallP[:, sl, 1, :], 1e-30, None, ALU.max))
                    ln(nc.vector.reciprocal(f, f))
                    gate = gN[:, t, :].rearrange("p (b h) -> p b h", b=3)[:, :, bass.ds(8 * G + 2 * (r // 4) + r % 2, 1)].rearrange("p b i -> p (b i)")
                    ln(nc.vector.tensor_tensor(f, f, gate, ALU.mult))
                    for br, (c0, c1) in enumerate(((0, ncmp), (16, 16 + nk), (272, 272 + nk))):
                        ins = nc.vector.tensor_scalar(Pp[sl][:, c0:c1], Pp[sl][:, c0:c1], f[:, br:br + 1], None, ALU.mult)
                    ins.then_inc(scaled, 1)

                def turned_out(r, G):
                    t, sl = r // 2 % 2, r % 2
                    ncmp = 7 if t == 0 else NCMP_P
                    dve.wait_ge(p_turned, 16 * G + r + 3)
                    dve.wait_ge(o_summed, 16 * G + r + 1)
                    nc.vector.tensor_copy(PC[sl][0:ncmp, :], ps[0:ncmp, SCORE_BANKS[r % 3] + 1, 384:512]).then_inc(pc_ready, 1)

                def take(r, G):
                    gp, chunk, t = r // 8, r // 4 % 2, r // 2 % 2
                    half = slice(64 * (r % 2), 64 * (r % 2) + 64)
                    dve.wait_ge(o_summed, 16 * G + r + 3)
                    nc.vector.tensor_copy(zT[half, bass.ds(4 * G + 2 * gp + chunk, 1), P * t:P * t + P],
                                          ps[half, 7, 0:P].rearrange("p (i q) -> p i q", i=1)).then_inc(o_taken, 1)

                dve.wait_ge(gates_ready, 1)
                with dve.Fori(0, 2) as G:
                    ln = Links(G, 16 * 4, 2)
                    maxima(0, G, ln)
                    maxima(1, G, ln)
                    for r in range(16):
                        scale(r, G, ln)
                        turned_out(r, G)
                        if r > 0:
                            take(r - 1, G)
                        if r < 14:
                            maxima(r + 2, G, ln)
                    take(15, G)
                    ln.end()

                col = lambda c, n=1: smallS[:, c:c + n]
                def norm_keys(i, b2, ln):
                    dve.wait_ge(s_ksq, 2 * i + b2 + 1)
                    sq = KT[:, :, :].rearrange("p g n -> p (g n)").rearrange("p (n d) -> p n d", d=HD)
                    ln(nc.vector.tensor_reduce(col(16, 48), sq, AX.X, ALU.add))
                    nc.vector.tensor_scalar(col(16, 48), col(16, 48), 1.0 / HD, EPS, ALU.mult, ALU.add).then_inc(s_kvar, 1)
                    dve.wait_ge(s_kstd, 2 * i + b2 + 1)
                    ln(nc.vector.reciprocal(col(64, 48), col(64, 48)))
                    k = kr[b2][:, :, :].rearrange("p n (g d) -> p (n g) d", d=HD)
                    nc.vector.tensor_tensor(k, k, col(64, 48).rearrange("p (g i) -> p g i", i=1).to_broadcast([P, 48, HD]),
                                            ALU.mult).then_inc(s_kn, 1)

                def pair(i, ln, last=False):
                    gate = gR[:, bass.ds(i, 1), :].rearrange("p i b -> p (i b)")
                    sc = S[:, 1600:1600 + NCMP_S]
                    dve.wait_ge(s_cscored, i + 1)
                    dve.wait_ge(bias_ready, 3)
                    ln(nc.vector.tensor_tensor(sc, ps[:, 3, 64:64 + NCMP_S], biasc[:, 0:NCMP_S], ALU.add))
                    ln(nc.vector.tensor_reduce(col(9), sc, AX.X, ALU.max))
                    nc.vector.tensor_scalar(col(0), col(9), -1.0, None, ALU.mult).then_inc(s_cmax, 1)
                    dve.wait_ge(s_cexp, i + 1)
                    ln(nc.vector.reciprocal(col(2), col(1)))
                    ln(nc.vector.tensor_scalar(sc, sc, col(2), None, ALU.mult))
                    ln(nc.vector.scalar_tensor_tensor(out=sc, in0=sc, scalar=1.17549435e-38, in1=sc, op0=ALU.is_ge, op1=ALU.mult))
                    quad = sc[:, 3:59].rearrange("p (j k) -> p j k", k=4)
                    E = col(112, 14)
                    ln(nc.vector.tensor_reduce(E, quad[:, :, 1:4], AX.X, ALU.add))
                    ln(nc.vector.scalar_tensor_tensor(out=E, in0=E, scalar=2.0, in1=quad[:, :, 0], op0=ALU.mult, op1=ALU.add))
                    ln(nc.vector.tensor_tensor(E, E, sc[:, 7:63].rearrange("p (j k) -> p j k", k=4)[:, :, 0], ALU.add))
                    ln(nc.vector.tensor_scalar(sc, sc, gate[:, 0:1], None, ALU.mult))
                    nc.vector.tensor_copy(col(157), col(9)).then_inc(imp_ready, 1)
                    dve.wait_ge(imp_summed, i + 1)
                    imp, J = ps[:, 7, 0:14], const[:, C_J:C_J + 14]
                    ln(nc.vector.tensor_reduce(col(10), imp, AX.X, ALU.min))
                    ln(nc.vector.scalar_tensor_tensor(out=col(126, 14), in0=imp, scalar=col(10), in1=J, op0=ALU.is_le, op1=ALU.mult))
                    ln(nc.vector.tensor_reduce(col(11), col(126, 14), AX.X, ALU.max))
                    ln(nc.vector.tensor_scalar(col(140, 14), J, col(11), NEG, ALU.is_equal, ALU.mult))
                    dve.wait_ge(s_scored, 2 * i + 3)
                    new = bnew[:, bass.ds(i, 1), :].rearrange("p i t -> p (i t)")
                    nc.vector.tensor_tensor(S[:, 1056:1568], ps[:, 2, :], bias[:, WIN:PAST], ALU.add)
                    ln(nc.vector.tensor_tensor(S[:, 1568:1600], ps[:, 3, NS:2 * NS], new, ALU.add))
                    ln(nc.vector.tensor_tensor(S[:, 1056:1060], S[:, 1056:1060], const[:, C_WIN:C_WIN + 4], ALU.add))
                    ln(nc.vector.tensor_reduce(col(156), S[:, 1056:1600], AX.X, ALU.max))
                    nc.vector.tensor_scalar(col(4), col(156), -1.0, None, ALU.mult).then_inc(s_max, 1)
                    nc.vector.tensor_tensor(S[:, 0:PAST], ps[:, 0:2, :].rearrange("p b n -> p (b n)"), bias[:, 0:PAST], ALU.add)
                    ln(nc.vector.tensor_tensor(S[:, PAST:1056], ps[:, 3, 0:NS], new, ALU.add))
                    dropped = S[:, 64:960].rearrange("p (j k) -> p j k", k=64)
                    mask = col(140, 14).rearrange("p (j i) -> p j i", i=1).to_broadcast([P, 14, 64])
                    ln(nc.vector.tensor_tensor(dropped, dropped, mask, ALU.add))
                    ln(nc.vector.tensor_reduce(col(155), S[:, 0:1056], AX.X, ALU.max))
                    nc.vector.tensor_scalar(col(3), col(155), -1.0, None, ALU.mult).then_inc(s_max, 1)
                    for k, (c0, c1) in enumerate(((1056, 1600), (0, 1056))):
                        dve.wait_ge(s_exp, 2 * i + k + 1)
                        f = col(8 - k)
                        ln(nc.vector.reciprocal(f, col(6 - k)))
                        ln(nc.vector.tensor_tensor(f, f, gate[:, 2 - k:3 - k], ALU.mult))
                        nc.vector.tensor_scalar(S[:, c0:c1], S[:, c0:c1], f, None, ALU.mult).then_inc(s_scaled, 1)
                    if not last:
                        norm_keys(i + 1, 0, ln)
                    dve.wait_ge(s_pv, i + 2)
                    ln(nc.vector.tensor_scalar(S[:, 0:64], ps[:, 6, 0:64], const[:, C_HALF:C_HALF + 1], None, ALU.mult))
                    nc.vector.scalar_tensor_tensor(out=S[:, 0:64], in0=ps[:, 6, 64:128], scalar=const[:, C_HALF + 1:C_HALF + 2],
                                                   in1=S[:, 0:64], op0=ALU.mult, op1=ALU.add).then_inc(s_o, 1)
                    dve.wait_ge(s_oturned, i + 1)
                    for b2 in range(2):
                        for pp in range(2):
                            src = ps[0:64, 7, P + 64 * b2:P + 64 * b2 + 64].rearrange("d (g t c p) -> d g c t p", t=NT, c=2, p=2)
                            dst = zT[64 * pp:64 * pp + 64, 0:8, bass.ds(NP_ + 8 * i + 4 * b2, NT)].rearrange("d (g c) t -> d g c t", c=2)
                            ins = nc.vector.tensor_copy(dst, src[:, :, :, :, pp])
                    ins.then_inc(s_done, 1)
                    if not last:
                        norm_keys(i + 1, 1, ln)

                for b2 in range(2):
                    norm_keys(0, b2, link)
                with dve.Fori(0, 3) as i:
                    ln = Links(i, 28, 3)
                    pair(i, ln)
                    ln.end()
                pair(3, link, True)
                for h in range(2):
                    dve.wait_ge(ohi_done, h + 1)
                    nc.vector.tensor_tensor(hL[:, 4 * h:4 * h + 4, :], zT[:, 4 * h:4 * h + 4, :], hH[:, 4 * h:4 * h + 4, :].bitcast(F32),
                                            ALU.subtract).then_inc(o_split, 1)
                out_stage(4, OUT1)

            dve.sem_inc(z_done, 2)
            dve.sem_inc(qvar_ready, 1)
            dve.sem_inc(pc_ready, 2)
            dve.sem_inc(xta_ready, 2)
            dve.sem_inc(xtd_ready, 2)
            dve.sem_inc(o_taken, 12)
            dve.sem_inc(zin_done, 2)
            dve.sem_inc(lo_done, 2)
            dve.sem_inc(h_done, 1)
            dve.sem_inc(hid_done, 1)
            dve.sem_inc(xupd_done, 2)
            dve.sem_inc(ada_done, 1)
            dve.wait_ge(rows_turned, 5)
            nc.vector.tensor_copy(vecA[:, 0:P], ps[:, 5, 0:P]).then_inc(vecs_ready, 1)
            nc.vector.tensor_copy(vecA[:, P:144], ps[:, 5, P:P + 16]).then_inc(vecs_ready, 1)
            nc.vector.tensor_copy(vecB[:, :], ps[:, 5, 256:256 + 64]).then_inc(vecs_ready, 1)
            nc.vector.tensor_copy(vecC[:, :], ps[:, 5, 384:384 + 4 * CW]).then_inc(vecs_ready, 1)
            dve.wait_ge(vecs_ready, 4)
            for u in range(ADA_UNITS):
                finish_ada(0, u, u, link)
            lower(0, 0)
            norm(0, True)
            lower(1, 1)
            ffn(0)
            norm(1, False)
            dve.wait_ge(mix_landed, MIX_LANDED)
            dve.wait_ge(const_landed, 16)
            for h in range(2):
                dve.wait_ge(ws_turned, h + 1)
                up = const[:, C_UP:C_UP + P].rearrange("p (i t) -> p i t", i=1).to_broadcast([P, 4, P])
                nc.vector.tensor_tensor(wT[:, 4 * h:4 * h + 4, :], ps[:, 4 + h, :].rearrange("p (g t) -> p g t", g=4), up, ALU.mult).then_inc(ws_ready, 1)
            blk = const[0:NS, C_BLK:C_BLK + NS].rearrange("p (i t) -> p i t", i=1).to_broadcast([NS, 8, NS])
            nc.vector.tensor_tensor(wS[:, :, :], wS[:, :, :], blk, ALU.mult).then_inc(ws_ready, 1)
            dve.wait_ge(st_turned, 1)
            for c in range(4):
                nc.vector.tensor_copy(cS[:, c, :, 0:30], ps[:, 6 + c // 2, 256 * (c % 2):256 * (c % 2) + 240].rearrange("p (b w) -> p b w", w=30)).then_inc(ws_ready, 1)
            even()
            norm(2, True)
            ffn(1)
            norm(3, True)
            ffn(2)
            norm(4, False)
            odd()
            norm(5, True)
            ffn(3)

        @block.tensor
        def _(pe):
            def product(bank, parity, block_, rhsH, rhsL, first, last):
                o = ps[:, bank, 0:T]
                h, l_ = wH[parity][:, block_:block_ + P], wL[parity][:, block_:block_ + P]
                nc.tensor.matmul(o, l_, rhsH, start=first, stop=False)
                nc.tensor.matmul(o, h, rhsL, start=False, stop=False)
                return nc.tensor.matmul(o, h, rhsH, start=False, stop=last)

            def unit(n, parity, banks, k0, k1, H, L, first, last, half=None):
                pe.wait_ge(lo_done, n + 3)
                for t in range(2):
                    for k in range(k0, k1):
                        if half is not None and t == 0 and k == 4:
                            pe.wait_ge(h_ready, half)
                        mm = product(banks + t, parity, (k - k0) * UW + t * P, H[:, k, :], L[:, k, :],
                                     first and k == k0, last and k == k1 - 1)
                mm.then_inc(unit_used, 1)

            def ada_unit(third, u, n, landed):
                pe.wait_ge(ada_landed[ada_slot[third, u]], landed)
                pe.wait_ge(mpart_ready, n + 1)
                for i in range(2):
                    for j in range(4):
                        k = 2 * j + i
                        mm = nc.tensor.matmul(ps[32 * j:32 * j + 32, 6, 0:UW], cT[:, k, :], ada[ada_slot[third, u]][:, k, :],
                                              start=(i == 0), stop=(i == 1), skip_group_check=True)
                mm.then_inc(ada_used, 1)

            def turn_ada(n):
                pe.wait_ge(mpart_ready, n + 2)
                pe.wait_ge(ada_done, n + 1)
                for c in range(2):
                    mm = nc.tensor.transpose(ps[:, 7, c * P:c * P + P], mpart[:, c * P:c * P + P], ident)
                mm.then_inc(ada_turned, 1)

            def sum_squares(k):
                third = ADA_AFTER_NORM[k]
                if third is not None:
                    ada_unit(third, 0, first_ada[third], count[third, 0])
                pe.wait_ge(sq_done, 4 * (k + 1))
                pe.wait_ge(ada_done, 1 + ADA_UNITS * ADA_BEFORE_NORM[k])
                for c in range(KD):
                    mm = nc.tensor.matmul(ps[:, 7, 0:T], ones[:, :], tmp[:, c, :], start=(c == 0), stop=(c == KD - 1))
                mm.then_inc(ms_ready, 1)
                if third is not None:
                    pe.wait_ge(var_ready, STAT_OF[k] + 1)
                    turn_ada(first_ada[third])

            def ffn(f):
                base = FFN_BASE[f]
                t1, t2 = ADA_IN_W1[f], ADA_IN_W2[f]
                pe.wait_ge(h_ready, 2 * NORM_OF[f] + 1)
                with pe.Fori(0, HALF_PAIRS) as j:
                    na, J = base + 2 * j, HALF_PAIRS * f + j
                    pe.wait_ge(silu_done, J + 1)
                    unit(na, 0, 0, 0, KD, hH, hL, True, True, 2 * NORM_OF[f] + 2)
                    if t1 is not None:
                        ada_unit(t1, 0, first_ada[t1] + 1 + j, count[t1, 0] + 16 * j + 16)
                    pe.wait_ge(h_done, J + 1)
                    unit(na + 1, 1, 2, 0, KD, hH, hL, True, True)
                    if t1 is not None:
                        turn_ada(first_ada[t1] + 1 + j)

                def pair(q, banks):
                    n = base + KF + 4 * q
                    pe.wait_ge(xupd_done, 4 * PAIR_STAGE[f] + q + 1)
                    for u in range(4):
                        pe.wait_ge(hid_done, HALF_PAIRS * (f + 1) + (1 if u == 3 else 0))
                        unit(n + u, u % 2, banks, W2CUT[u], W2CUT[u + 1], hidH, hidL, u == 0, u == 3)
                        if t2 is not None:
                            if u > 0:
                                turn_ada(first_ada[t2] + 3 * q + u - 1)
                            if u < 3:
                                per = 32 if u != 1 else 16
                                ada_unit(t2, u, first_ada[t2] + 3 * q + u, count[t2, u] + per * q)

                with pe.Fori(0, 2) as qq:
                    pair(2 * qq, 4)
                    pair(2 * qq + 1, 0)

            def even():
                def project(i, late):
                    for u in range(2):
                        if late:
                            pe.wait_ge(glu_ready, 2 * u + 2)
                            pe.wait_ge(zin_done, 2 * i + u - 1)
                        else:
                            pe.wait_ge(zin_done, 2 * i + u + 1)
                        unit(IN0 + 2 * i + u, u, 2 * u, 0, KD, hH, hL, True, True)

                def convolve(c):
                    for w in range(CW):
                        pe.wait_ge(diag_ready, c * CW + w + 1)
                        nc.tensor.matmul(ps[:, 6, NP_ * c:NP_ * c + NP_], diag[:, (c * CW + w) % DIAGS, :], cP[:, 2 + c, w:w + NP_],
                                         start=(w == 0), stop=(w == CW - 1), skip_group_check=True).then_inc(tap_summed, 1)

                pe.wait_ge(h_ready, 4)
                with pe.Fori(0, 2) as i:
                    project(i, False)
                with pe.Fori(2, 4) as i:
                    project(i, True)
                pe.wait_ge(pad_ready, 1)
                pe.wait_ge(glu_ready, 4)
                pe.wait_ge(ws_ready, 7)
                convolve(0)
                pe.wait_ge(vsq_done, 1)
                for c in range(4):
                    mm = nc.tensor.matmul(ps[:, 7, 0:T], ones[:, :], tmp[:, c, :], start=(c == 0), stop=(c == 3))
                mm.then_inc(ms_ready, 1)
                convolve(1)
                pe.wait_ge(v_ready, 4)
                for t in range(2):
                    for c in range(4):
                        mm = nc.tensor.transpose(ps[:, 4 + t, c * P:c * P + P], vT[:, c, t * P:t * P + P], ident)
                    mm.then_inc(v_turned, 1)
                for c in range(4):
                    mm = nc.tensor.transpose(ps[0:NS, 7, c * P:c * P + P], vT[:, c, NP_:T], ident)
                mm.then_inc(v_turned, 1)
                pe.wait_ge(vn_ready, 3)
                pe.wait_ge(ws_ready, 7)
                pe.wait_ge(glu_ready, 4)
                for c in range(4):
                    for h in range(2):
                        o, ch = ps[64 * h:64 * h + 64, c, :], slice(c * P + 64 * h, c * P + 64 * h + 64)
                        for t in range(2):
                            nc.tensor.matmul(o[:, t * P:t * P + P], vn[:, t, ch], wT[:, 2 * c + h, :], start=True, stop=True)
                        mm = nc.tensor.matmul(o[:, NP_:T], vns[:, ch], wS[:, 2 * c + h, :], start=True, stop=True)
                mm.then_inc(gate_summed, 1)
                for c in range(4):
                    nc.tensor.transpose(ps[0:30, 4, c * P:c * P + P], cP[:, c, NP_:30 + NP_], ident)
                    mm = nc.tensor.transpose(ps[0:NS, 5, c * P:c * P + P], gS[:, c, :], ident)
                mm.then_inc(glu_turned, 1)
                pe.wait_ge(conv_ready, 1)
                for c in range(4):
                    mm = nc.tensor.matmul(ps[:, 7, 0:T], ones[:, :], acc[:, c, :], start=(c == 0), stop=(c == 3))
                mm.then_inc(mean_ready, 1)
                pe.wait_ge(csq_done, 1)
                for c in range(4):
                    mm = nc.tensor.matmul(ps[:, 7, 0:T], ones[:, :], tmp[:, 4 + c, :], start=(c == 0), stop=(c == 3))
                mm.then_inc(ms_ready, 1)
                pe.wait_ge(mixed, 2)
                out_stage(OUT0, 1)

            def out_stage(first, stage):
                with pe.Fori(0, 2) as i:
                    for u in range(2):
                        pe.wait_ge(xupd_done, 4 * stage + 2 * i + u + 1)
                        unit(first + 2 * i + u, u, 4 - 4 * u, 0, KD, hH, hL, True, True)

            def odd():
                pe.wait_ge(h_ready, 10)
                pe.wait_ge(ada_done, 6 * ADA_UNITS + 1)
                for k in range(KD):
                    mm = nc.tensor.matmul(ps[0:48, 6, 0:T], gw[:, k, :], tmp[:, k, :], start=(k == 0), stop=(k == KD - 1))
                mm.then_inc(gates_summed, 1)
                with pe.Fori(0, 5) as i:
                    for u in range(2):
                        pe.wait_ge(z_done, 2 * i + u + 1)
                        unit(IN1 + 2 * i + u, u, 2 * u, 0, KD, hH, hL, True, True)
                pe.wait_ge(gate_ready, 1)
                for t in range(2):
                    nc.tensor.transpose(ps[:, 6, 48 * t:48 * t + 48], gT[:, P * t:P * t + P], const[0:48, C_ID:C_ID + 48])
                for br in range(3):
                    mm = nc.tensor.matmul(ps[:, 6, P + NS * br:P + NS * br + NS], gcon[0:48, G_HEAD + P * br:G_HEAD + P * br + P],
                                          gT[:, NP_:T], start=True, stop=True)
                mm.then_inc(gate_turned, 1)
                pe.wait_ge(z_done, 12)
                for t in range(3):
                    if t == 2:
                        pe.wait_ge(kv_rows, 1)
                    n, cols = (P, slice(t * P, t * P + P)) if t < 2 else (NS, slice(NP_, T))
                    for c in range(12):
                        mm = nc.tensor.transpose(ps[0:n, 3 * (t % 2) + c // 4, c % 4 * P:c % 4 * P + P], zT[:, ROW_CHUNKS[c], cols], ident)
                    mm.then_inc(kv_turned, 1)
                pe.wait_ge(kv_rows, 3)
                nc.tensor.matmul(ps[0:16, 7, 0:REL], table[:, :], hotb[:, 0:REL], start=True, stop=True).then_inc(rel_summed, 1)
                pe.wait_ge(gates_ready, 1)
                nc.tensor.matmul(ps[:, 6, 0:224], TE[:, :], const[:, C_OH:C_OH + 224], start=True, stop=True).then_inc(bias_summed, 1)
                pe.wait_ge(bias_ready, 3)
                pe.wait_ge(rel_ready, 1)

                def turn_pairs(b, v):
                    for n in range(4):
                        pe.wait_ge(cre_ready, 8 * b + 4 * v + n + 9)
                        pe.wait_ge((xta_ready, xtd_ready)[n % 2], 4 * b + 2 * v + n // 2 + 1)
                        for g in range(4):
                            mm = nc.tensor.transpose(ps[:, n, P * g:P * g + P], cre[:, n, g, :, :].rearrange("p s d -> p (s d)"), ident)
                        mm.then_inc(cre_turned, 1)

                def step(b, v, last, norm_too=False):
                    pe.wait_ge(xta_ready, 4 * b + 2 * v + 4)
                    pe.wait_ge(xtd_ready, 4 * b + 2 * v + 4)
                    compress(2 * b + v + 2, v, NCMP_S, XTs[v][:, :, :], b + 1 + v, b + 1, 1, None if last else (b + 1, v))
                    if norm_too:
                        pe.wait_ge(qvar_ready, 2 * b + v + 1)
                        pe.wait_ge(qsq_ready, 2 * b + v + 1)
                        nc.tensor.matmul(ps[:, 7, 0:T], const[:, C_BD:C_BD + P], rowt[:, 0, :], start=True, stop=True).then_inc(qsum_ready, 1)

                def compress(s, v, n, pairs, turned, keys, copies, ahead=None):
                    for c in range(16):
                        mm = nc.tensor.matmul(ps[:, 4, 0:4 * n], w1c[:, v, c, :], pairs[:, :, c:c + 8 * n - 7:8],
                                              start=(c == 0), stop=(c == 15))
                    mm.then_inc(chid_summed, 1)
                    if v == 1:
                        if copies == 1:
                            hold(pe, "pe", kc_ready, keys)
                            hold(pe, "pe", ck_ready, keys + 1)
                        else:
                            pe.wait_ge(ck_ready, 1)
                        flat = kcn[0:n, :, :, :].rearrange("p g i d -> p (g i d)")
                        for g in range(4 if copies == 2 else 2):
                            mm = nc.tensor.transpose(ps[:, 6, P * g:P * g + n], flat[:, P * g:P * g + P], const[0:n, C_ID:C_ID + n])
                        mm.then_inc(ck_turned, 1)
                    if ahead is not None:
                        turn_pairs(*ahead)
                    pe.wait_ge(chid_ready, s + 1)
                    if turned is not None:
                        pe.wait_ge(ck_ready, turned)
                        pe.wait_ge(ckv_taken, s)
                    for g in range(4):
                        mm = nc.tensor.matmul(ps[0:n, 5, HD * g:HD * g + HD], hid[:, g, 0:n], w2c[:, v, :], start=True, stop=True)
                    mm.then_inc(ckv_summed, 1)

                turn_pairs(0, 0)
                pe.wait_ge(xp_ready, 1)
                xp = XTs[1][:, 0:2, :].rearrange("p a (b n) -> p (a b) n", n=P)
                compress(0, 0, NCMP_P, xp[:, 0:4, :], None, 0, 2)
                compress(1, 1, NCMP_P, xp[:, 4:8, :], 1, 0, 2)
                turn_pairs(0, 1)
                with pe.Fori(0, NB - 2) as b:
                    step(b, 0, False, True)
                    step(b, 1, False, True)
                step(NB - 2, 0, False)
                step(NB - 2, 1, False)
                step(NB - 1, 0, True)
                step(NB - 1, 1, True)

                def scores(r, G):
                    gp, chunk, t, sl = r // 8, r // 4 % 2, r // 2 % 2, r % 2
                    nk, ncmp, off = (P, 7, P) if t == 0 else (2 * P, NCMP_P, 0)
                    half = slice(64 * sl, 64 * sl + 64)
                    if r % 8 == 0:
                        pe.wait_ge(group_ready, 16 * G + 8 * gp + 8)
                    pe.wait_ge(exped, 16 * G + earlier(r))
                    pe.wait_ge(pc_ready, 16 * G + earlier(r))
                    A, B = ps[:, SCORE_BANKS[r % 3], :], ps[:, SCORE_BANKS[r % 3] + 1, :]
                    q = qS[gp][half, chunk, P * t:P * t + P]
                    anti = const[:, C_ANTI:C_ANTI + P]
                    rel = Ur[:, bass.ds(8 * G + 2 * (r // 4) + r % 2, 1), :].rearrange("p i n -> p (i n)")
                    nc.tensor.matmul(A[:, 0:16 + nk], q, KS[gp][half, 0:16 + nk], start=True, stop=False, skip_group_check=True)
                    nc.tensor.matmul(A[:, 16:16 + nk], anti, rel[:, off:off + nk], start=False, stop=False, skip_group_check=True)
                    c0 = off + 31
                    nc.tensor.matmul(A[:, 0:ncmp], anti, rel[:, c0:c0 + 16 * ncmp - 15:16], start=False, stop=True, skip_group_check=True)
                    nc.tensor.matmul(B[:, 16:16 + nk], q, KS[gp][half, 272:272 + nk], start=True, stop=False, skip_group_check=True)
                    nc.tensor.matmul(B[:, 16:16 + nk], anti, rel[:, off:off + nk], start=False, stop=True, skip_group_check=True).then_inc(scored, 1)

                def turn(r, G):
                    t, sl = r // 2 % 2, r % 2
                    ncmp = 7 if t == 0 else NCMP_P
                    pe.wait_ge(scaled, 16 * G + r + 1)
                    pe.wait_ge(pt_ready, 16 * G + r + 2)
                    for k, c in enumerate((16, 272) if t == 0 else (16, 144, 272, 400)):
                        nc.tensor.transpose(ps[:, 4, P * k:P * k + P], Pp[r % 3][:, c:c + P], ident)
                    nc.tensor.transpose(ps[0:ncmp, SCORE_BANKS[r % 3] + 1, 384:512], Pp[r % 3][:, 0:ncmp], ident).then_inc(p_turned, 1)

                def weigh(r, G):
                    gp, t, sl = r // 8, r // 2 % 2, r % 2
                    ncmp, tiles = (7, 1) if t == 0 else (NCMP_P, 2)
                    pe.wait_ge(pt_ready, 16 * G + r + 3)
                    pe.wait_ge(pc_ready, 16 * G + r + 3)
                    pe.wait_ge(o_taken, 16 * G + r + 11)
                    o = ps[64 * sl:64 * sl + 64, 7, 0:P]
                    nc.tensor.matmul(o, VC[gp][0:ncmp, :], PC[sl][0:ncmp, :], start=True, stop=False, skip_group_check=True)
                    for br in range(2):
                        for k in range(tiles):
                            c = P * (tiles * br + k)
                            mm = nc.tensor.matmul(o, VS[gp][:, k, br, :], PT[sl][:, c:c + P], start=False,
                                                  stop=(br == 1 and k == tiles - 1), skip_group_check=True)
                    mm.then_inc(o_summed, 1)

                pe.wait_ge(u_landed, 16)
                with pe.Fori(0, 2) as G:
                    scores(0, G)
                    scores(1, G)
                    for r in range(16):
                        if r < 14:
                            scores(r + 2, G)
                        turn(r, G)
                        if r > 0:
                            weigh(r - 1, G)
                    weigh(15, G)

                with pe.Fori(0, 4) as i:
                    pe.wait_ge(s_small, 3 * i + 3)
                    for j in range(4):
                        b2, G = divmod(j, 2)
                        mm = nc.tensor.matmul(ps[32 * j:32 * j + 32, 3, 64:64 + NCMP_S], QS[:, b2, G, :], KCs[:, b2, G, 0:NCMP_S],
                                              start=True, stop=True, skip_group_check=True)
                    mm.then_inc(s_cscored, 1)
                    for b2 in range(2):
                        pe.wait_ge(s_kn, 2 * i + b2 + 1)
                        for k in range(6):
                            pe.wait_ge(kt_ready, 12 * i + 6 * b2 + k + 1)
                            G = k // 3
                            for n in range(4):
                                mm = nc.tensor.transpose(ps[:, 4 + k % 2, P * n:P * n + P], kr[b2][:, 4 * (k % 3) + n, P * G:P * G + P], ident)
                            mm.then_inc(kt_turned, 1)
                        if b2 == 1:
                            pe.wait_ge(imp_ready, i + 1)
                            nc.tensor.matmul(ps[:, 7, 0:14], const[:, C_GRP:C_GRP + P], smallS[:, 112:126], start=True,
                                             stop=True).then_inc(imp_summed, 1)
                        pe.wait_ge(kt_ready, 12 * i + 6 * b2 + 8)
                        pe.wait_ge(s_cmax, i + 1)
                        for G in range(2):
                            rows_ = slice(64 * b2 + 32 * G, 64 * b2 + 32 * G + 32)
                            q = QS[:, b2, G, :]
                            for dst, src in ((ps[rows_, 0, :], KT[:, G, 0:512]), (ps[rows_, 1, :], KT[:, G, 512:1024]),
                                             (ps[rows_, 2, :], KT[:, G, 1024:1536]), (ps[rows_, 3, 0:NS], zT[:, 8 + G, NP_:T]),
                                             (ps[rows_, 3, NS:2 * NS], zT[:, 10 + G, NP_:T])):
                                mm = nc.tensor.matmul(dst, q, src, start=True, stop=True, skip_group_check=True)
                        mm.then_inc(s_scored, 1)
                    cols = [1056 + P * n for n in range(4)] + [P * n for n in range(8)]
                    for k in range(4):
                        if k < 2:
                            pe.wait_ge(s_scaled, 2 * i + k + 1)
                        if k >= 2:
                            pe.wait_ge(s_pready, 5 * i + k - 1)
                        if k < 3:
                            for n in range(4):
                                c = cols[4 * k + n]
                                mm = nc.tensor.transpose(ps[:, 4 + k % 2, P * n:P * n + P], S[:, c:c + P], ident)
                        else:
                            for n, (c, w) in enumerate(((PAST, NS), (1568, NS), (1600, NCMP_S))):
                                mm = nc.tensor.transpose(ps[0:w, 5, P * n:P * n + P], S[:, c:c + w], ident)
                        mm.then_inc(s_pturned, 1)
                    pe.wait_ge(s_pready, 5 * i + 5)
                    for b2 in range(2):
                        pe.wait_ge(v_landed[b2], 144 * i + 144)
                    for j in range(4):
                        b2, G = divmod(j, 2)
                        o, rows_ = ps[32 * j:32 * j + 32, 6, 0:P], slice(32 * j, 32 * j + 32)
                        for n in range(12):
                            nc.tensor.matmul(o, PTs[:, n, rows_], vr[b2][:, (n + 8) % 12, P * G:P * G + P], start=(n == 0), stop=False, skip_group_check=True)
                        for n in range(2):
                            v = 768 + 512 * n + P * G
                            nc.tensor.matmul(o, PTs[0:NS, 12 + n, rows_], kvs[:, v:v + P], start=False, stop=False, skip_group_check=True)
                        mm = nc.tensor.matmul(o, PTs[0:NCMP_S, 14, rows_], vcs[:, b2, 2 * G:2 * G + 2, :].rearrange("p g d -> p (g d)"),
                                              start=False, stop=True, skip_group_check=True)
                    mm.then_inc(s_pv, 1)
                    pe.wait_ge(s_o, i + 1)
                    nc.tensor.transpose(ps[:, 7, P:2 * P], S[:, 0:P], ident).then_inc(s_oturned, 1)
                pe.wait_ge(o_split, 2)
                out_stage(OUT1, 4)

            pe.sem_inc(p_turned, 2)
            pe.sem_inc(o_summed, 2)
            pe.sem_inc(cre_turned, 4)
            pe.sem_inc(kt_turned, 12)
            pe.sem_inc(s_scored, 1)
            pe.sem_inc(s_pv, 1)
            pe.sem_inc(unit_used, 2)
            pe.sem_inc(ada_turned, 1)
            pe.wait_ge(const_landed, 16)
            pe.wait_ge(c_landed, 32)
            nc.tensor.transpose(ps[:, 4, 0:KD * NC], rows[0:KD * NC, 4, :], const[0:KD * NC, C_ID:C_ID + KD * NC]).then_inc(rows_turned, 1)
            pe.wait_ge(ones_ready, 3)
            pe.wait_ge(cT_ready, 1)
            for u in range(ADA_UNITS):
                ada_unit(0, u, u, count[0, u])
                if u == 0:
                    pe.wait_ge(setup_landed, SETUP_LANDED)
                    for k, n, col in ((0, P, 0), (1, 16, P), (2, 64, 256), (3, 4 * CW, 384)):
                        nc.tensor.transpose(ps[:, 5, col:col + n], rows[0:n, k, :], const[0:n, C_ID:C_ID + n]).then_inc(rows_turned, 1)
                turn_ada(u)
                c = u - 3
                if 0 <= c < KD:
                    pe.wait_ge(x_landed, 32)
                    if c >= 4:
                        pe.wait_ge(x_ready, c - 3)
                    for t in range(2):
                        nc.tensor.transpose(ps[:, c % 4, t * P:t * P + P], xin[:, t, c * P:c * P + P], ident)
                    nc.tensor.transpose(ps[:, c % 4, NP_:T], xin[0:NS, 2, c * P:c * P + P], const[0:NS, C_ID:C_ID + NS]).then_inc(x_turned, 1)
            sum_squares(0)
            ffn(0)
            sum_squares(1)
            pe.wait_ge(mix_landed, MIX_LANDED)
            for g in range(8):
                mm = nc.tensor.transpose(ps[:, 4 + g // 4, g % 4 * P:g % 4 * P + P], wsn[:, g, :], ident)
                if g % 4 == 3:
                    mm.then_inc(ws_turned, 1)
            for c in range(4):
                if c == 2:
                    pe.wait_ge(var_ready, STAT_OF[1] + 1)
                for h in range(2):
                    at_ = 256 * (c % 2) + 120 * h
                    mm = nc.tensor.transpose(ps[:, 6 + c // 2, at_:at_ + 120], stn[:, h, c * P:c * P + P], const[0:120, C_ID:C_ID + 120])
            mm.then_inc(st_turned, 1)
            even()
            sum_squares(2)
            ffn(1)
            sum_squares(3)
            ffn(2)
            sum_squares(4)
            pe.wait_ge(late_landed, 16 * LATE)
            nc.tensor.transpose(ps[:, 5, 0:32], perow[:, :], const[0:32, C_ID:C_ID + 32]).then_inc(pe_turned, 1)
            pe.wait_ge(pe_copied, 1)
            pe.wait_ge(w1_landed, 32)
            for v in range(2):
                for c in range(16):
                    mm = nc.tensor.matmul(ps[:, 5, 32 + v:33 + v], w1c[:, v, c, :], peT[:, 16 * v + c:16 * v + c + 1],
                                          start=(c == 0), stop=(c == 15))
            mm.then_inc(peb_summed, 1)
            odd()
            sum_squares(5)
            ffn(3)
            pe.wait_ge(xupd_done, 26)
            for t in range(3):
                if t == 2:
                    pe.wait_ge(y_rows, 1)
                n, cols = (P, slice(t * P, t * P + P)) if t < 2 else (NS, slice(NP_, T))
                for c in range(KD):
                    mm = nc.tensor.transpose(ps[0:n, 2 * (t % 2) + c // 4, c % 4 * P:c % 4 * P + P], xT[:, c, cols], ident)
                mm.then_inc(y_turned, 1)


NORM_OF = [0, 2, 3, 5]
STAT_OF = [0, 1, 4, 5, 6, 7]
STAT_V, STAT_LN = 2, 3
PAIR_STAGE = [0, 2, 3, 5]
ADA_AFTER_NORM = [1, None, 3, 5, None, None]
ADA_BEFORE_NORM = [1, 3, 3, 5, 6, 6]


_OUTS = [(1, 256, 1024), (8, 4, 1024), (1, 256, 1, 2, 4, 64), (8, 4, 1, 2, 4, 64), (1, 256, 1, 2, 4, 64), (8, 4, 1, 2, 4, 64),
         (1, 1, 256, 2, 4, 64), (1, 8, 512, 2, 4, 64), (1, 1, 30, 512), (1, 8, 30, 512), (1, 8, 4, 512)]


def kernel(**inputs):
    import concourse.bacc as bacc
    from concourse.bass_utils import run_bass_kernel_spmd as run

    nc = bacc.Bacc("TRN2", target_bir_lowering=False, num_devices=1)
    arrays, args = {}, {}
    data = {name: np.ascontiguousarray(v) for name, v in inputs.items()}
    data.update(zip(("consts", "gcon", "hot", "causal"), shape_constants()))
    for name, v in data.items():
        arrays[f"in_{name}_dram"] = v
        args[name] = nc.dram_tensor(f"in_{name}_dram", v.shape, mybir.dt.from_np(v.dtype), kind="ExternalInput").ap()
    outs = [nc.dram_tensor(f"out_{i}_dram", shape, F32, kind="ExternalOutput").ap() for i, shape in enumerate(_OUTS)]
    emit(nc, args, outs)
    r = run(nc, [arrays], core_ids=[0])
    return tuple(r.results[0][f"out_{i}_dram"] for i in range(len(_OUTS)))
```
